# Optimizing a Trainium2 kernel written in Bass

```python
import jax
import jax.numpy as jnp
from jax import lax
import numpy as np

D_MODEL = 1024
BATCH = 1
SEQ = 256
DEPTH = 4
DEC_BATCH = 8
DEC_SEQ = 8
PAST_LEN = 2048
PAGE_SIZE = 128

N_MIXERS = 4
EPS = 1e-6
CHUNK = 128
D_A = D_MODEL
A_GROUPS = 8
A_GDIM = D_A // A_GROUPS
POOL_WINDOWS = (2, 4, 8, 16)
POOL_GROUPS = len(POOL_WINDOWS)
POOL_GDIM = D_MODEL // POOL_GROUPS
POOL_BUF = max(POOL_WINDOWS) - 1
D_C = D_MODEL
CONV_WIDTH = 31
CONV_BUF = CONV_WIDTH - 1
GDN_HEADS = 8
GDN_DK = 128
GDN_DV = 128
GDN_CONV = 4
GDN_BUF = GDN_CONV - 1
GDN_QKV = GDN_HEADS * (2 * GDN_DK + GDN_DV)
GDN_CHUNK = 64
D_FF = 2816
FFN_CONV = 3
FFN_BUF = FFN_CONV - 1
N_A = (DEPTH + 3) // 4
N_B = (DEPTH + 2) // 4
N_C = (DEPTH + 1) // 4
N_D = DEPTH // 4

kernel_name = 'hybrid_chunkmlp_pool_conformer_gdn_step'

F32 = jnp.float32

def rmsnorm(x, g):
    xf = x.astype(F32)
    y = xf * lax.rsqrt(jnp.mean(xf * xf, axis=-1, keepdims=True) + EPS)
    return y.astype(x.dtype) * g

def layernorm(x, g, b):
    xf = x.astype(F32)
    mu = jnp.mean(xf, axis=-1, keepdims=True)
    var = jnp.mean(jnp.square(xf - mu), axis=-1, keepdims=True)
    return ((xf - mu) * lax.rsqrt(var + EPS)).astype(x.dtype) * g + b

def l2norm(x):
    xf = x.astype(F32)
    return (xf * lax.rsqrt(jnp.sum(xf * xf, axis=-1, keepdims=True) + EPS)).astype(x.dtype)

def causal_dwconv(x, buf, w):
    k, c = w.shape
    t = x.shape[1]
    xp = jnp.concatenate([buf.astype(x.dtype), x], axis=1)
    y = lax.conv_general_dilated(xp, w[:, None, :].astype(x.dtype), window_strides=(1,),
                                 padding='VALID', dimension_numbers=('NWC', 'WIO', 'NWC'),
                                 feature_group_count=c)
    return y, xp[:, t:]

def chunk_mlp(h, start_pos, w_in, b_in, ln_g, ln_b, w_s, b_s, w_out):
    bsz, t, _ = h.shape
    u, v = jnp.split(jax.nn.gelu(h @ w_in + b_in), 2, axis=-1)
    v = layernorm(v, ln_g, ln_b)
    n_chunks = -(-t // CHUNK)
    vp = jnp.pad(v, ((0, 0), (0, n_chunks * CHUNK - t), (0, 0)))
    vp = vp.reshape(bsz, n_chunks, CHUNK, A_GROUPS, A_GDIM)
    causal = jnp.tril(jnp.ones((CHUNK, CHUNK), dtype=bool))
    ws = jnp.where(causal, w_s, 0.0)
    mixed = jnp.einsum('gij,bnjgc->bnigc', ws, vp) + b_s.T[None, None, :, :, None]
    mixed = mixed.reshape(bsz, n_chunks * CHUNK, D_A)[:, :t]
    last_start = ((start_pos + t - 1) // CHUNK) * CHUNK - start_pos
    return (u * mixed) @ w_out, v[:, last_start:]

def multiscale_pool(h, buf, start_pos, w_grp, scale):
    bsz, t, _ = h.shape
    hp = jnp.concatenate([buf.astype(h.dtype), h], axis=1)
    cs = jnp.pad(jnp.cumsum(hp.astype(F32), axis=1), ((0, 0), (1, 0), (0, 0)))
    pos = start_pos + jnp.arange(t)
    outs = []
    for gi, win in enumerate(POOL_WINDOWS):
        sl = slice(gi * POOL_GDIM, (gi + 1) * POOL_GDIM)
        hi = cs[:, POOL_BUF + 1:POOL_BUF + 1 + t, sl]
        lo = cs[:, POOL_BUF + 1 - win:POOL_BUF + 1 - win + t, sl]
        cnt = jnp.minimum(pos + 1, win).astype(F32)[None, :, None]
        outs.append((hi - lo) / cnt)
    pooled = jnp.concatenate(outs, axis=-1).astype(h.dtype) - h
    pooled = pooled.reshape(bsz, t, POOL_GROUPS, POOL_GDIM)
    y = jnp.einsum('btgc,gcd->btgd', pooled, w_grp).reshape(bsz, t, D_MODEL) * scale
    return y, hp[:, t:]

def conformer_conv(h, buf, w_pw1, b_pw1, w_dw, b_dw, ln_g, ln_b, w_pw2, b_pw2):
    a, gt = jnp.split(h @ w_pw1 + b_pw1, 2, axis=-1)
    z = a * jax.nn.sigmoid(gt)
    z, new_buf = causal_dwconv(z, buf, w_dw)
    z = jax.nn.silu(layernorm(z + b_dw, ln_g, ln_b))
    return z @ w_pw2 + b_pw2, new_buf

def chunk_gated_delta(q, k, v, g, beta, s0):
    bsz, t, nh, _ = q.shape
    dv = v.shape[-1]
    c = GDN_CHUNK if t >= GDN_CHUNK else t
    n = -(-t // c)
    pad = n * c - t

    def blocks(a):
        a = jnp.pad(a.astype(F32), ((0, 0), (0, pad)) + ((0, 0),) * (a.ndim - 2))
        a = a.reshape((bsz, n, c) + a.shape[2:])
        return jnp.moveaxis(a, (1, 3), (0, 2))

    qb, kb, vb, gb, bb = blocks(q), blocks(k), blocks(v), blocks(g), blocks(beta)
    gc = jnp.cumsum(gb, axis=-1)
    incl = jnp.tril(jnp.ones((c, c), dtype=bool))
    strict = jnp.tril(jnp.ones((c, c), dtype=bool), k=-1)
    decay = jnp.exp(jnp.where(incl, gc[..., :, None] - gc[..., None, :], -jnp.inf))
    k_beta = kb * bb[..., None]
    lmat = jnp.where(strict, jnp.einsum('nbhid,nbhjd->nbhij', k_beta, kb) * decay, 0.0)
    rhs = jnp.concatenate([vb * bb[..., None], k_beta * jnp.exp(gc)[..., None]], axis=-1)
    sol = lax.linalg.triangular_solve(lmat + jnp.eye(c, dtype=F32), rhs, left_side=True,
                                      lower=True, unit_diagonal=True)
    u, w = sol[..., :dv], sol[..., dv:]
    qk = jnp.where(incl, jnp.einsum('nbhid,nbhjd->nbhij', qb, kb) * decay, 0.0)

    def step(s, xs):
        q_c, k_c, u_c, w_c, g_c, qk_c = xs
        v_new = u_c - jnp.einsum('bhck,bhkv->bhcv', w_c, s)
        o_c = (jnp.einsum('bhck,bhkv->bhcv', q_c * jnp.exp(g_c)[..., None], s)
               + jnp.einsum('bhij,bhjv->bhiv', qk_c, v_new))
        g_last = g_c[..., -1]
        s = (s * jnp.exp(g_last)[..., None, None]
             + jnp.einsum('bhck,bhcv->bhkv', k_c * jnp.exp(g_last[..., None] - g_c)[..., None], v_new))
        return s, o_c

    s_final, o = lax.scan(step, s0.astype(F32), (qb, kb, u, w, gc, qk))
    o = jnp.moveaxis(o, (0, 2), (1, 3)).reshape(bsz, n * c, nh, dv)[:, :t]
    return o.astype(q.dtype), s_final.astype(s0.dtype)

def gated_deltanet(h, conv_buf, s0, w_qkv, w_conv, w_ab, dt_bias, a_log, w_g, o_norm_g, w_out):
    bsz, t, _ = h.shape
    qkv, new_buf = causal_dwconv(h @ w_qkv, conv_buf, w_conv)
    qkv = jax.nn.silu(qkv)
    hk = GDN_HEADS * GDN_DK
    q = l2norm(qkv[..., :hk].reshape(bsz, t, GDN_HEADS, GDN_DK)) * (GDN_DK ** -0.5)
    k = l2norm(qkv[..., hk:2 * hk].reshape(bsz, t, GDN_HEADS, GDN_DK))
    v = qkv[..., 2 * hk:].reshape(bsz, t, GDN_HEADS, GDN_DV)
    ab = (h @ w_ab).astype(F32)
    beta = jax.nn.sigmoid(ab[..., :GDN_HEADS])
    g = -jnp.exp(a_log.astype(F32)) * jax.nn.softplus(ab[..., GDN_HEADS:] + dt_bias.astype(F32))
    o, s_new = chunk_gated_delta(q, k, v, g, beta, s0)
    gate = jax.nn.silu(h @ w_g).reshape(bsz, t, GDN_HEADS, GDN_DV)
    o = rmsnorm(o, o_norm_g) * gate
    return o.reshape(bsz, t, GDN_HEADS * GDN_DV) @ w_out, new_buf, s_new

def conv_ffn(h, buf, w_up, w_dw, b_dw, w_down):
    a, b = jnp.split(h @ w_up, 2, axis=-1)
    a, new_buf = causal_dwconv(a, buf, w_dw)
    return (jax.nn.silu(a + b_dw) * b) @ w_down, new_buf

def trunk(x, start_pos, pool_buf, conv_buf, gdnc_buf, gdns, ffn_buf, p):
    chunk_v, pool_new, conv_new, gdnc_new, gdns_new, ffn_new = [], [], [], [], [], []
    for i in range(DEPTH):
        j = i // N_MIXERS
        kind = i % N_MIXERS
        h = rmsnorm(x, p['norm_mix_g'][i])
        if kind == 0:
            y, vr = chunk_mlp(h, start_pos, p['a_w_in'][j], p['a_b_in'][j], p['a_ln_g'][j],
                              p['a_ln_b'][j], p['a_w_s'][j], p['a_b_s'][j], p['a_w_out'][j])
            chunk_v.append(vr)
        elif kind == 1:
            y, nb = multiscale_pool(h, pool_buf[j], start_pos, p['b_w_grp'][j], p['b_scale'][j])
            pool_new.append(nb)
        elif kind == 2:
            y, nb = conformer_conv(h, conv_buf[j], p['c_w_pw1'][j], p['c_b_pw1'][j], p['c_w_dw'][j],
                                   p['c_b_dw'][j], p['c_ln_g'][j], p['c_ln_b'][j],
                                   p['c_w_pw2'][j], p['c_b_pw2'][j])
            conv_new.append(nb)
        else:
            y, nb, ns = gated_deltanet(h, gdnc_buf[j], gdns[j], p['d_w_qkv'][j], p['d_w_conv'][j],
                                       p['d_w_ab'][j], p['d_dt_bias'][j], p['d_a_log'][j],
                                       p['d_w_g'][j], p['d_o_norm_g'][j], p['d_w_out'][j])
            gdnc_new.append(nb)
            gdns_new.append(ns)
        x = x + y
        h = rmsnorm(x, p['norm_ffn_g'][i])
        y, fb = conv_ffn(h, ffn_buf[i], p['f_w_up'][i], p['f_w_dw'][i], p['f_b_dw'][i], p['f_w_down'][i])
        ffn_new.append(fb)
        x = x + y
    x = rmsnorm(x, p['norm_final_g'])
    return (x, jnp.stack(chunk_v), jnp.stack(pool_new), jnp.stack(conv_new), jnp.stack(gdnc_new),
            jnp.stack(gdns_new), jnp.stack(ffn_new))

def setup_inputs(seed: int = 0) -> dict:
    key = jax.random.key(seed)
    ks = list(jax.random.split(key, 48))

    def nrm(shape, scale):
        return scale * jax.random.normal(ks.pop(), shape, F32)

    def gain(shape):
        return 1.0 + nrm(shape, 0.05)

    D = D_MODEL
    H = GDN_HEADS
    dt = jnp.exp(jax.random.uniform(ks.pop(), (N_D, H), F32, np.log(1e-3), np.log(1e-1)))
    a_init = jax.random.uniform(ks.pop(), (N_D, H), F32, 1.0, 16.0)
    return {
        'x_prompt': nrm((BATCH, SEQ, D), 1.0),
        'x_sample': nrm((DEC_BATCH, DEC_SEQ, D), 1.0),
        'state_pool': nrm((N_B, DEC_BATCH, POOL_BUF, D), 1.0),
        'state_conv': nrm((N_C, DEC_BATCH, CONV_BUF, D_C), 0.5),
        'state_gdn_conv': nrm((N_D, DEC_BATCH, GDN_BUF, GDN_QKV), 1.0),
        'state_gdn_S': nrm((N_D, DEC_BATCH, H, GDN_DK, GDN_DV), 0.3),
        'state_ffn_conv': nrm((DEPTH, DEC_BATCH, FFN_BUF, D_FF), 1.0),
        'norm_mix_g': gain((DEPTH, D)),
        'norm_ffn_g': gain((DEPTH, D)),
        'norm_final_g': gain((D,)),
        'a_w_in': nrm((N_A, D, 2 * D_A), D ** -0.5),
        'a_b_in': nrm((N_A, 2 * D_A), 0.02),
        'a_ln_g': gain((N_A, D_A)),
        'a_ln_b': nrm((N_A, D_A), 0.02),
        'a_w_s': nrm((N_A, A_GROUPS, CHUNK, CHUNK), CHUNK ** -0.5),
        'a_b_s': gain((N_A, A_GROUPS, CHUNK)),
        'a_w_out': nrm((N_A, D_A, D), 0.5 * D_A ** -0.5),
        'b_w_grp': nrm((N_B, POOL_GROUPS, POOL_GDIM, POOL_GDIM), POOL_GDIM ** -0.5),
        'b_scale': 0.3 + nrm((N_B, D), 0.05),
        'c_w_pw1': nrm((N_C, D, 2 * D_C), D ** -0.5),
        'c_b_pw1': nrm((N_C, 2 * D_C), 0.02),
        'c_w_dw': nrm((N_C, CONV_WIDTH, D_C), CONV_WIDTH ** -0.5),
        'c_b_dw': nrm((N_C, D_C), 0.02),
        'c_ln_g': gain((N_C, D_C)),
        'c_ln_b': nrm((N_C, D_C), 0.02),
        'c_w_pw2': nrm((N_C, D_C, D), 0.5 * D_C ** -0.5),
        'c_b_pw2': nrm((N_C, D), 0.02),
        'd_w_qkv': nrm((N_D, D, GDN_QKV), D ** -0.5),
        'd_w_conv': nrm((N_D, GDN_CONV, GDN_QKV), 0.5),
        'd_w_ab': nrm((N_D, D, 2 * H), 0.5 * D ** -0.5),
        'd_dt_bias': dt + jnp.log(-jnp.expm1(-dt)),
        'd_a_log': jnp.log(a_init),
        'd_w_g': nrm((N_D, D, H * GDN_DV), D ** -0.5),
        'd_o_norm_g': gain((N_D, GDN_DV)),
        'd_w_out': nrm((N_D, H * GDN_DV, D), 0.5 * (H * GDN_DV) ** -0.5),
        'f_w_up': nrm((DEPTH, D, 2 * D_FF), D ** -0.5),
        'f_w_dw': nrm((DEPTH, FFN_CONV, D_FF), FFN_CONV ** -0.5),
        'f_b_dw': nrm((DEPTH, D_FF), 0.02),
        'f_w_down': nrm((DEPTH, D_FF, D), 0.5 * D_FF ** -0.5),
    }

def reference(x_prompt, x_sample, state_pool, state_conv, state_gdn_conv, state_gdn_S, state_ffn_conv,
              norm_mix_g, norm_ffn_g, norm_final_g,
              a_w_in, a_b_in, a_ln_g, a_ln_b, a_w_s, a_b_s, a_w_out,
              b_w_grp, b_scale,
              c_w_pw1, c_b_pw1, c_w_dw, c_b_dw, c_ln_g, c_ln_b, c_w_pw2, c_b_pw2,
              d_w_qkv, d_w_conv, d_w_ab, d_dt_bias, d_a_log, d_w_g, d_o_norm_g, d_w_out,
              f_w_up, f_w_dw, f_b_dw, f_w_down):
    p = dict(norm_mix_g=norm_mix_g, norm_ffn_g=norm_ffn_g, norm_final_g=norm_final_g,
             a_w_in=a_w_in, a_b_in=a_b_in, a_ln_g=a_ln_g, a_ln_b=a_ln_b, a_w_s=a_w_s, a_b_s=a_b_s,
             a_w_out=a_w_out, b_w_grp=b_w_grp, b_scale=b_scale,
             c_w_pw1=c_w_pw1, c_b_pw1=c_b_pw1, c_w_dw=c_w_dw, c_b_dw=c_b_dw, c_ln_g=c_ln_g,
             c_ln_b=c_ln_b, c_w_pw2=c_w_pw2, c_b_pw2=c_b_pw2,
             d_w_qkv=d_w_qkv, d_w_conv=d_w_conv, d_w_ab=d_w_ab, d_dt_bias=d_dt_bias, d_a_log=d_a_log,
             d_w_g=d_w_g, d_o_norm_g=d_o_norm_g, d_w_out=d_w_out,
             f_w_up=f_w_up, f_w_dw=f_w_dw, f_b_dw=f_b_dw, f_w_down=f_w_down)
    bp = x_prompt.shape[0]
    dt = x_prompt.dtype
    (y_prompt, p_chunk_v, p_pool, p_conv, p_gdn_conv, p_gdn_S, p_ffn) = trunk(
        x_prompt, 0,
        jnp.zeros((N_B, bp, POOL_BUF, D_MODEL), dt),
        jnp.zeros((N_C, bp, CONV_BUF, D_C), dt),
        jnp.zeros((N_D, bp, GDN_BUF, GDN_QKV), dt),
        jnp.zeros((N_D, bp, GDN_HEADS, GDN_DK, GDN_DV), dt),
        jnp.zeros((DEPTH, bp, FFN_BUF, D_FF), dt), p)
    (y_sample, s_chunk_v, s_pool, s_conv, s_gdn_conv, s_gdn_S, s_ffn) = trunk(
        x_sample, PAST_LEN, state_pool, state_conv, state_gdn_conv, state_gdn_S, state_ffn_conv, p)
    return (y_prompt, y_sample, p_chunk_v, s_chunk_v, p_pool, s_pool, p_conv, s_conv,
            p_gdn_conv, s_gdn_conv, p_gdn_S, s_gdn_S, p_ffn, s_ffn)


_drawn_inputs = setup_inputs


def setup_inputs(seed=0):
    import zlib

    import numpy as np

    out = dict(_drawn_inputs(seed))
    spreads = {}
    factors = {'a_ln_b': 2.744, 'c_b_dw': 4.032, 'c_ln_b': 7.648, 'd_o_norm_g': 4.71, 'f_b_dw': 4.227}
    for name, (base, spread) in spreads.items():
        noise = np.random.default_rng([zlib.crc32(name.encode()), seed]).standard_normal(out[name].shape)
        drawn = base * np.exp(spread * noise) if base else spread * noise
        out[name] = jnp.asarray(drawn.astype(out[name].dtype))
    for name, factor in factors.items():
        out[name] = (out[name] * factor).astype(out[name].dtype)
    return out
```

```python
from contextlib import ExitStack

import concourse.bass as bass
from concourse import mybir

F32 = mybir.dt.float32
F32R = mybir.dt.float32r
ACT = mybir.ActivationFunctionType
ALU = mybir.AluOpType

P = 128
D = 1024
KT = D // P
SEQ, NB, DEC = 256, 8, 8
NT = SEQ + NB * DEC
DEPTH = 4
DFF = 2816
FT = DFF // P
PARTS = ((0, 6), (6, 11), (11, 17), (17, 22))
EPS = 1e-6
SLOTS = 4
ARENA = 10984
CONVW = 31
PETAPS = 14
POOLW = (2, 4, 8, 16)
CHUNK = 64
CHUNKS = SEQ // CHUNK
TW = 3 * P
HEADS = 8
UNIT = KT * P

def padded(h):
    return h + SEQ + NB * (h + DEC)

FW, PW, CW, QW = padded(2), padded(15), padded(30), padded(3)

def _columns():
    at, out = 0, {}
    for name, n in (("gain", 9 * KT), ("a_b", 16), ("a_lg", 8), ("a_lb", 8), ("b_scale", 8),
                    ("c_b1", 16), ("c_dw", CONVW * 8), ("c_bdw", 8), ("c_lg", 8), ("c_lb", 8),
                    ("c_b2", 8), ("d_cw", 24 * 4), ("d_on", 1), ("d_dt", 1), ("d_al", 1), ("f", DEPTH * FT * 4), ("inv", 64)):
        out[name] = at
        at += n
    return out, at

COL, NCOL = _columns()

PHASES = []
for _l, _first in enumerate(([("a_in", 16, 8 * P), ("a_out", 8, 8 * P)],
                             [("b_grp", 8, 2 * P)],
                             [("c_pw1", 16, 8 * P), ("c_pw2", 8, 8 * P)],
                             [("d_ab", 4, 2 * P), ("d_qk", 16, 8 * P), ("d_vg", 16, 8 * P),
                              ("d_out", 8, 8 * P)])):
    PHASES += [(n, _l, u, c) for n, u, c in _first]
    PHASES += [("f_up", _l, 2 * FT, 8 * P), ("f_down", _l, 4 * KT, 0)]
START, _u = {}, 0
for _n, _l, _c, _w in PHASES:
    START[_n, _l] = _u
    _u += _c
UNITS = _u


def cols_of(u):
    for n, l, c, w in PHASES:
        if START[n, l] <= u < START[n, l] + c:
            return w or down_cols(u - START[n, l])
    return 0


def down_cols(k):
    a, b = PARTS[k % 4]
    return (b - a) * P


def htile(layer, ffn):
    return layer * (KT + FT) + (KT if ffn else 0)


def padded_at(h):
    return h + SEQ


class Steps:

    def __init__(self, eng, sem):
        self.eng, self.sem, self.n, self.off = eng, sem, 0, 0

    def mark(self, ins):
        ins.then_inc(self.sem, 1)
        self.n += 1

    def wait(self, but=0):
        self.eng.wait_ge(self.sem, self.off + (self.n - but))

    def enter(self, b, first, per):
        self.at, self.per = self.n, per
        self.off = b * per
        self.n -= first * per

    def leave(self, first, count):
        self.n += first * self.per
        assert self.n - self.at == self.per, (self.n - self.at, self.per)
        self.n += (count - 1) * self.per
        self.off = 0


def trunk_kernel(nc, t, out, layers=DEPTH):
    ctx = ExitStack()
    with ctx:
        def sb(name, shape, dt=F32):
            return ctx.enter_context(nc.sbuf_tensor(name, shape, dt))

        def sem(name):
            return ctx.enter_context(nc.semaphore(name))

        bank = [ctx.enter_context(nc.psum_tensor(f"bank{i}", [P, 512], F32)) for i in range(8)]
        acc = bank[:4]
        stat = bank[4]
        mixb = bank[5:8]

        raw = [sb(f"raw{i}", [P, UNIT]) for i in range(SLOTS)]
        whi = [sb(f"whi{i}", [P, UNIT], F32R) for i in range(SLOTS)]
        wlo = [sb(f"wlo{i}", [P, UNIT], F32R) for i in range(SLOTS)]
        X = sb("X", [P, KT * NT])
        Gh = sb("Gh", [P, KT * NT], F32R)
        Gl = sb("Gl", [P, KT * NT], F32R)
        Hh = sb("Hh", [P, FT * NT], F32R)
        spare = (FT - KT) * NT
        Hh_spare = nc.alloc_sbuf_tensor_at("Hh_spare", [P, spare], F32, offset=nc.sbuf_base - 4 * spare)
        Hl = sb("Hl", [P, FT * NT], F32R)
        Hl_spare = nc.alloc_sbuf_tensor_at("Hl_spare", [P, spare], F32, offset=nc.sbuf_base - 4 * spare)
        par = sb("par", [P, NCOL])
        R = sb("R", [P, NT])
        sd = sb("sd", [P, NT])
        ssq = sb("ssq", [P, NT])
        sq = [sb(f"sq{i}", [P, TW]) for i in range(2)]
        hbuf = [sb(f"hbuf{i}", [P, NT]) for i in range(2)]
        tmp = [sb(f"tmp{i}", [P, NT]) for i in range(2)]
        tmb = [sb(f"tmb{i}", [P, NT]) for i in range(2)]
        fpad = [sb(f"fpad{i}", [P, QW]) for i in range(2)]
        ftap = [sb(f"ftap{i}", [P, QW]) for i in range(2)]
        fsil = [sb(f"fsil{i}", [P, QW]) for i in range(2)]
        fst = sb("fst", [P, 24 * 24])
        fnew = sb("fnew", [P, 24 * 27])
        ones = sb("ones", [P, P])
        ident = sb("ident", [P, P])
        eps = sb("eps", [P, 1])
        M = sb("M", [P, ARENA])

        raw_full = [sem(f"raw_full{i}") for i in range(SLOTS)]
        hi_ready, lo_ready, unit_done = sem("hi_ready"), sem("lo_ready"), sem("unit_done")
        evac = sem("psum_evacuated")
        g_hi, g_ready = sem("g_hi"), sem("g_ready")
        sq_ready, ssq_ready = sem("sq_ready"), sem("ssq_ready")
        stat_done, std_ready = sem("stat_done"), sem("std_ready")
        h_mid, h_hi, h_ready = sem("h_mid"), sem("h_hi"), sem("h_ready")
        tap_ready, sil_ready = sem("tap_ready"), sem("sil_ready")
        par_in, x_in, fst_in, mix_in = sem("par_in"), sem("x_in"), sem("fst_in"), sem("mix_in")
        consts = sem("consts")
        dve_steps = sem("dve_steps")
        ln_sum, ln_stat, ln_std = sem("ln_sum"), sem("ln_stat"), sem("ln_std")
        gelu_done = sem("gelu_done")
        v_ready, vT_done, vtok_ready, mixed = sem("v_ready"), sem("vT_done"), sem("vtok_ready"), sem("mixed")
        mix_read = sem("mix_read")
        sig_ready, z_ready, ca_done = sem("sig_ready"), sem("z_ready"), sem("ca_done")
        conv_in, pool_in = sem("conv_in"), sem("pool_in")
        diag_ready, conv_done, conv_read = sem("diag_ready"), sem("conv_done"), sem("conv_read")
        gdn_in, rows_stored, rows_in = sem("gdn_in"), sem("rows_stored"), [sem("rows_in0"), sem("rows_in1")]
        states_in = [sem("states_in0"), sem("states_in1")]
        conv_taps, tanh_ready, silu_ready = sem("conv_taps"), sem("tanh_ready"), sem("silu_ready")
        l2sq_ready, l2sums = sem("l2sq_ready"), sem("l2sums")
        ab_v, ab_a, ab_t = sem("ab_vector"), sem("ab_scalar"), sem("ab_tensor")
        kq_ready, kb_ready, qe_ready, eg_ready = sem("kq_ready"), sem("kb_ready"), sem("qe_ready"), sem("eg_ready")
        diff_ready, decay_ready, kk_done, kv_turned = sem("diff_ready"), sem("decay_ready"), sem("kk_done"), sem("kv_turned")
        scores_ready, lt_ready, qt_ready = sem("scores_ready"), sem("lt_ready"), sem("qt_ready")
        kv_scaled, tt_ready, t_turned, t_ready = sem("kv_scaled"), sem("tt_ready"), sem("t_turned"), sem("t_ready")
        lt_done, b_ready, tb_done, inv_ready = sem("lt_done"), sem("b_ready"), sem("tb_done"), sem("inv_ready")
        w_done, u_done, w_ready = sem("w_done"), sem("u_done"), sem("w_ready")
        sv_done, vs_ready, vs_turned, vns_ready = sem("sv_done"), sem("vs_ready"), sem("vs_turned"), sem("vns_ready")
        vx_ready, sdec_ready, sx_done, ss_ready = sem("vx_ready"), sem("sdec_ready"), sem("sx_done"), sem("ss_ready")
        vn_ready, ws_done, su_done, s_ready = sem("vn_ready"), sem("ws_done"), sem("su_done"), sem("s_ready")
        o_done, osq_ready, osum_done, osd_ready = sem("o_done"), sem("osq_ready"), sem("osum_done"), sem("osd_ready")
        y_ready, y_stored, fout, stored = sem("y_ready"), sem("y_stored"), sem("fout"), sem("stored")

        def col(name, i=0):
            at = COL[name] + i if isinstance(i, int) else i + COL[name]
            return par[:, at:at + 1] if isinstance(at, int) else par[:, bass.ds(at, 1)]

        def tile_of(buf, m, width=NT):
            return buf[:, m * width:(m + 1) * width] if isinstance(m, int) else buf[:, bass.ds(m * width, width)]

        def prompt(ap):
            return ap[:, 0:SEQ]

        def sample(ap, b=NB):
            return ap[:, SEQ:NT].rearrange("p (b t) -> p b t", b=b)

        def in_pad(ap, h, first, n):
            at = padded_at(h)
            return ap[:, at:at + NB * (h + DEC)].rearrange("p (b t) -> p b t", b=NB)[:, :, first:first + n]

        V3, U3 = M[:, 0:KT * NT], M[:, KT * NT:2 * KT * NT]
        at = 2 * KT * NT
        wsT = M[:, at:at + 1024]
        wbd = M[0:64, at + 1024:at + 1536]
        bsb = M[:, at + 1536:at + 2560]
        vtok = [M[:, at + 2560 + 384 * i:at + 2560 + 384 * (i + 1)] for i in range(2)]
        hp = [M[:, PW * i:PW * (i + 1)] for i in range(2)]
        lv = [M[:, PW * (2 + i):PW * (3 + i)] for i in range(2)]
        pst = M[:, 4 * PW:4 * PW + KT * NB * 15]
        pnew = M[:, 4 * PW + KT * NB * 15:4 * PW + KT * (2 * NB + 1) * 15]
        Z3 = M[:, 0:KT * NT]
        zpad = M[:, KT * NT:KT * NT + KT * CW]
        DVETAPS = CONVW - PETAPS
        diag = [M[:, 7296 + i * PETAPS * P:7296 + (i + 1) * PETAPS * P] for i in range(2)]

        room = [[M, 0, ARENA], [Hh_spare, 0, spare], [Hl_spare, 0, spare]]

        def place(n):
            for piece in room:
                if piece[1] + n <= piece[2]:
                    piece[1] += n
                    return piece[0][:, piece[1] - n:piece[1]]
            raise ValueError(f"no room for {n}: {room}")

        def two(n):
            return [place(n), place(n)]

        qk = place(2 * HEADS * NT)
        dmask = place(6 * P + 2 * TW + NB)
        mlev = [dmask[:, i * P:(i + 1) * P] for i in range(6)]
        mstrict, mincl = dmask[:, 6 * P:6 * P + TW], dmask[:, 6 * P + TW:6 * P + 2 * TW]
        mseq = dmask[:, 6 * P + 2 * TW:]
        SS = two(NB * P)
        Sst = [sd[:, 0:P], sd[:, P:2 * P]]
        bx = two(NB * P)
        kh, kb, qh, vf, kdec = two(TW), two(TW), two(TW), two(TW), two(TW)
        LT, TT, kw = two(TW), two(TW), two(TW)
        WQ = two(2 * NT)
        VN = two(CHUNKS * P)
        VNs = [ssq[:, 0:P], ssq[:, P:2 * P]]
        vsT = two(2 * NB * DEC)
        gate = [hb[:, :] for hb in hbuf]
        cols = place(3 * 5 * HEADS)
        dc = place(8)
        rqb, rkb, gcb = ([bx[x][:, NT * i:NT * (i + 1)] for x in range(2)] for i in range(3))
        beb = [a[:, :] for a in tmp]
        Tm = [bx[x][:, 0:TW] for x in range(2)]
        VX = bx
        Bm, vp = kb, qh
        dec, QT, eg = fsil, [a[:, 0:NT] for a in ftap], tmb
        gtanh = [a[:, 0:NT] for a in sq]
        AB, XG, G1, RW, RN = kh[0], kh[1], LT[0], LT[1], TT[0]
        gT, KD = TT[1], kw[0]
        rnc = kw[1][:, 0:48]
        zeroed = [a[:, NT:TW] for a in (kh + vf)] + VN + VNs + [G1, RW, sq[0][:, NT:TW], sq[1][:, NT:TW]] \
            + [f[:, 0:3] for f in fpad]
        scr_g = nc.dram_tensor("scr_g", [HEADS, 2, NT], F32).ap()
        scr_n = nc.dram_tensor("scr_n", [2 * HEADS, NT], F32).ap()
        GDN_STORED = 18 + 1 + 2 * HEADS
        ZEROS = 11 + len(zeroed)
        BETA, GC, KDEC, EG = 0, 32, 64, 96
        C_BETA, C_GC, C_KDEC, C_EG, C_BEG = (HEADS * i for i in range(5))

        def tile3(ap):
            return ap.rearrange("p (n t) -> p n t", n=3)

        def bcast(ap, n, w):
            return ap.rearrange("p (n t) -> p n t", n=1).to_broadcast([P, n, w])

        def sampled(ap, n=DEC):
            return ap.rearrange("p (b t) -> p b t", b=NB)

        G_READY, RW_READY, RN_READY, ROWS_READY = 3, 4, 5, 6
        GT_READY, RW_READY_A = 5, 7
        PAIR_STEPS = 46
        block = ctx.enter_context(nc.Block())
        NORMS = 2 * layers
        phases = [p for p in PHASES if p[1] < layers]
        LAST = START[phases[-1][0], phases[-1][1]] + phases[-1][2]

        @block.sync
        def _(sp):
            sp.dma_start(par[:, :], t["par"]).then_inc(par_in, 16)
            sp.dma_start(X[:, :], t["x"]).then_inc(x_in, 16)

            def load(name, l, b, k):
                u = b * 4 + (START[name, l] + k)
                if not isinstance(u, int) or u >= SLOTS:
                    sp.wait_ge(lo_ready, u - (SLOTS - 1))
                arr = t[name][l] if name[0] == "f" else t[name]
                if name == "f_down":
                    a, z = PARTS[k][0] * P, PARTS[k][1] * P
                    src = arr[b, :, a:z] if isinstance(b, int) else \
                        arr[bass.ds(b, 1), :, a:z].rearrange("a p n -> (a p) n")
                else:
                    z, a = arr.shape[-1], 0
                    src = arr[b * 4 + k, :, :] if isinstance(b, int) else \
                        arr[bass.ds(b * 4 + k, 1), :, :].rearrange("a p n -> (a p) n")
                sp.dma_start(raw[k][:, 0:z - a], src).then_inc(raw_full[k], 16)

            def gdn_stores():
                sp.wait_ge(ab_v, ROWS_READY)
                sp.dma_start(scr_g[:, 0, :], RW[GC:GC + HEADS, 0:NT]).then_inc(rows_stored, 16)
                sp.dma_start(scr_g[:, 1, :], RW[BETA:BETA + HEADS, 0:NT]).then_inc(rows_stored, 16)
                sp.dma_start(scr_n, RN[0:2 * HEADS, 0:NT]).then_inc(rows_stored, 16)

            def gdn_state_stores(b):
                for x in range(2):
                    h = b * 2 + x
                    sp.wait_ge(ss_ready, h + 1)
                    sp.wait_ge(par_in, 16)
                    for name, buf in (("gdn_Sp", Sst[x]), ("gdn_Ss", SS[x])):
                        dst = out[name][h] if isinstance(h, int) else \
                            out[name][bass.ds(h, 1), :, :].rearrange("a p n -> (a p) n")
                        sp.dma_start(dst, buf).then_inc(stored, 16)

            def gdn_pair_loads(b):
                for k in range(SLOTS):
                    load("d_vg", 3, b, k)
                if isinstance(b, int):
                    gdn_stores()
                else:
                    gdn_state_stores(b - 1)
                for x in range(2):
                    h = b * 2 + x
                    if isinstance(b, int):
                        if x == 0:
                            sp.wait_ge(rows_stored, 48)
                        srcs = scr_n[2 * h:2 * h + 2, :].rearrange("r n -> (r n)"), \
                            scr_g[h, 0, :], scr_g[h, 1, :], t["d_S"][h]
                    else:
                        sp.wait_ge(h_ready, h + (htile(3, False) - 1))
                        sp.wait_ge(stored, b * 64 + 16 * 18)
                        sp.wait_ge(par_in, 16)
                        srcs = scr_n[bass.ds(h * 2, 2), :].rearrange("r n -> (r n)"), \
                            scr_g[bass.ds(h, 1), 0, :].rearrange("a n -> (a n)"), \
                            scr_g[bass.ds(h, 1), 1, :].rearrange("a n -> (a n)"), \
                            t["d_S"][bass.ds(h, 1), :, :].rearrange("a p n -> (a p) n")
                    sp.dma_start(bx[x][:, 0:2 * NT], srcs[0].partition_broadcast(P)).then_inc(rows_in[x], 16)
                    sp.dma_start(gcb[x], srcs[1].partition_broadcast(P)).then_inc(rows_in[x], 16)
                    sp.dma_start(beb[x], srcs[2].partition_broadcast(P)).then_inc(rows_in[x], 16)
                    sp.dma_start(SS[x], srcs[3]).then_inc(states_in[x], 16)

            for name, l, n, w in phases:
                first = 0
                if name == "a_in":
                    for k in range(SLOTS):
                        load(name, l, 0, k)
                    first = 1
                    sp.dma_start(wsT, t["a_wsT"]).then_inc(mix_in, 16)
                    sp.dma_start(wbd, t["a_wbd"]).then_inc(mix_in, 16)
                    sp.dma_start(bsb, t["a_bs"].partition_broadcast(P)).then_inc(mix_in, 16)
                if name == "d_ab":
                    sp.wait_ge(unit_done, START["d_ab", 3])
                    sp.wait_ge(fout, 48)
                    sp.dma_start(dmask, t["d_mask"]).then_inc(gdn_in, 16)
                    sp.dma_start(fst[:, :], t["d_st"]).then_inc(gdn_in, 16)
                if name == "d_vg":
                    gdn_pair_loads(0)
                    with sp.Fori(1, 4) as b:
                        gdn_pair_loads(b)
                    continue
                if name == "d_out":
                    for k in range(SLOTS):
                        load(name, l, 0, k)
                    first = 1
                    sp.wait_ge(silu_ready, 24)
                    sp.dma_start(out["gdn_conv"], fnew[:, :]).then_inc(stored, 16)
                    gdn_state_stores(3)
                if name == "f_up":
                    if l > 0:
                        sp.wait_ge(fout, 16 * l)
                    sp.dma_start(fst[:, 0:FT * 16], t["f_st"][l]).then_inc(fst_in, 16)
                with sp.Fori(first, n // 4) as b:
                    for k in range(SLOTS):
                        load(name, l, b, k)
                if name == "f_up":
                    if l == 0:
                        sp.wait_ge(unit_done, START["f_up", 0] + 1)
                        sp.dma_start(out["chunk_v"], V3.rearrange("p (m t) -> p m t", t=NT)[:, :, 128:NT])\
                            .then_inc(stored, 16)
                        if layers > 1:
                            sp.wait_ge(stored, 16)
                            sp.dma_start(pst, t["b_st"]).then_inc(pool_in, 16)
                    if l == 1:
                        sp.wait_ge(unit_done, START["f_up", 1] + 1)
                        sp.dma_start(out["pool"], pnew).then_inc(stored, 16)
                        if layers > 2:
                            sp.wait_ge(stored, 32)
                            for m in range(KT):
                                sp.dma_start(in_pad(tile_of(zpad, m, CW), 30, 0, 30), t["c_st"][m])\
                                    .then_inc(conv_in, 16)
                    if l == 2:
                        sp.wait_ge(unit_done, START["f_up", 2] + 1)
                        for m in range(KT):
                            z = tile_of(zpad, m, CW)
                            sp.dma_start(out["conv_p"][m], z[:, SEQ:SEQ + 30]).then_inc(stored, 16)
                            sp.dma_start(out["conv_s"][m], in_pad(z, 30, DEC, 30)).then_inc(stored, 16)
                        if layers > 3:
                            sp.wait_ge(stored, 32 + 16 * 16)
                if name == "f_down":
                    sp.wait_ge(h_mid, htile(l, True) + FT)
                    sp.dma_start(out["ffn"][l], fnew[:, 0:FT * 18]).then_inc(fout, 16)
            for m in range(KT):
                sp.wait_ge(y_ready, m + 1)
                sp.dma_start(out["y"][:, m * NT:(m + 1) * NT], tile_of(X, m)).then_inc(y_stored, 16)
            sp.wait_ge(y_stored, 16 * KT)
            sp.wait_ge(fout, 16 * layers)
            sp.wait_ge(stored, 16 * (1, 2, 18, GDN_STORED)[layers - 1])

        @block.gpsimd
        def _(pool):
            pool.memset(ones[:, :], 1.0).then_inc(consts, 1)
            pool.memset(eps[:, :], EPS).then_inc(consts, 1)
            pool.memset(ident[:, :], 0.0).then_inc(consts, 1)
            pool.wait_ge(consts, 3)
            pool.affine_select(out=ident[:, :], in_=ident[:, :], compare_op=ALU.not_equal, fill=1.0,
                               base=0, pattern=[[-1, P]], channel_multiplier=1).then_inc(consts, 1)
            for i in range(2):
                pool.memset(fpad[i][:, :], 0.0).then_inc(consts, 1)

            def split_lo(u, k, w):
                pool.wait_ge(hi_ready, u + 1)
                if not isinstance(u, int) or u >= SLOTS:
                    pool.wait_ge(unit_done, u - (SLOTS - 1))
                pool.tensor_tensor(wlo[k][:, 0:w], raw[k][:, 0:w], whi[k][:, 0:w].bitcast(F32),
                                   ALU.subtract).then_inc(lo_ready, 1)

            def conv_body(b):
                for i in range(2):
                    m = b * 2 + i
                    for k in range(2 * i, 2 * i + 2):
                        split_lo(b * 4 + (START["c_pw1", 2] + k), k, UNIT)
                    if not isinstance(b, int):
                        pool.wait_ge(conv_done, m - 1)
                    at = m * CONVW + (COL["c_dw"] + DVETAPS)
                    w = par[:, at:at + PETAPS] if isinstance(m, int) else par[:, bass.ds(at, PETAPS)]
                    pool.tensor_tensor(diag[i].rearrange("p (k c) -> p k c", c=P), bcast(ident[:, :], PETAPS, P),
                                       w.rearrange("p (k c) -> p k c", c=1).to_broadcast([P, PETAPS, P]),
                                       ALU.mult).then_inc(diag_ready, 1)

            def gdn_pair(b):
                u0 = START["d_vg", 3]
                for x in range(2):
                    h = b * 2 + x
                    pool.wait_ge(kq_ready, h + 1)
                    pool.tensor_tensor(kb[x][:, 0:NT], kh[x][:, 0:NT], beb[x], ALU.mult).then_inc(kb_ready, 1)
                    pool.wait_ge(eg_ready, h + 1)
                    pool.tensor_tensor(WQ[x][:, 0:NT], qh[x][:, 0:NT], eg[x][:, :], ALU.mult).then_inc(qe_ready, 1)
                for x in range(2):
                    h = b * 2 + x
                    pool.wait_ge(scores_ready, h + 1)
                    pool.tensor_tensor(LT[x][:, 0:NT], LT[x][:, 0:NT], mstrict[:, 0:NT], ALU.mult).then_inc(lt_ready, 1)
                for x in range(2):
                    pool.tensor_tensor(QT[x], QT[x], mincl[:, 0:NT], ALU.mult).then_inc(qt_ready, 1)
                for k in range(4):
                    split_lo(b * 4 + (u0 + 4 + k), k, UNIT)
                for x in range(2):
                    h = b * 2 + x
                    pool.wait_ge(sv_done, h + 1)
                    last = sampled(eg[x][:, SEQ:NT])[:, :, DEC - 1:DEC].to_broadcast([P, NB, P])
                    pool.tensor_tensor(sampled(SS[x]), sampled(SS[x]), last, ALU.mult).then_inc(sdec_ready, 1)
                for x in range(2):
                    h = b * 2 + x
                    pool.wait_ge(vns_ready, h + 1)
                    pool.tensor_tensor(sampled(VX[x]), bcast(VNs[x], NB, P),
                                       mseq.rearrange("p (b t) -> p b t", t=1).to_broadcast([P, NB, P]),
                                       ALU.mult).then_inc(vx_ready, 1)

            for name, l, n, w in phases:
                u0, first = START[name, l], 0
                if name == "a_in":
                    for k in range(4):
                        split_lo(k, k, w)
                    first = 1
                    pool.wait_ge(mix_in, 48)
                    for ap, width in ((wsT, 128), (wbd, 64)):
                        v = ap.rearrange("p (g i) -> p g i", i=width)
                        pool.affine_select(out=v, in_=v, compare_op=ALU.is_ge, fill=0.0, base=0,
                                           pattern=[[0, KT], [1, width]], channel_multiplier=-1)\
                            .then_inc(consts, 1)
                if name == "d_out":
                    first = 1
                if name == "d_vg":
                    for k in range(4):
                        split_lo(u0 + k, k, UNIT)
                    gdn_pair(0)
                    with pool.Fori(1, 4) as b:
                        gdn_pair(b)
                    continue
                if name == "c_pw1":
                    pool.wait_ge(par_in, 16)
                    conv_body(0)
                    with pool.Fori(1, 4) as b:
                        conv_body(b)
                    continue
                with pool.Fori(first, n // 4) as b:
                    for k in range(4):
                        split_lo(b * 4 + (u0 + k), k, w or down_cols(k))
                if name == "d_ab":
                    pool.wait_ge(stored, 16 * 18)
                    pool.wait_ge(std_ready, 7)
                    for ap in zeroed:
                        pool.memset(ap, 0.0).then_inc(consts, 1)
                if name == "f_up" and l in (0, 1) and l + 1 < layers:
                    pool.wait_ge(stored, 16 * (l + 1))
                    if l == 0:
                        for i in range(2):
                            pool.memset(hp[i][:, 0:15], 0.0).then_inc(consts, 1)
                    else:
                        pool.memset(zpad.rearrange("p (m c) -> p m c", c=CW)[:, :, 0:30], 0.0).then_inc(consts, 1)

        @block.tensor
        def _(pe):
            def unit(u, k, hh, hl, dst, tiles, start=True, stop=True, ready=None):
                pe.wait_ge(hi_ready, u + 1)
                pe.wait_ge(lo_ready, u + 1)
                for n, kt in enumerate(tiles):
                    if ready:
                        pe.wait_ge(ready[0], ready[1] + kt + 1)
                    h, lo = tile_of(hh, kt), tile_of(hl, kt)
                    wh, wl = whi[k][:, n * P:(n + 1) * P], wlo[k][:, n * P:(n + 1) * P]
                    nc.tensor.matmul(dst, wh, h, start=start and n == 0, stop=False)
                    nc.tensor.matmul(dst, wh, lo, start=False, stop=False)
                    ins = nc.tensor.matmul(dst, wl, h, start=False, stop=stop and n == len(tiles) - 1)
                ins.then_inc(unit_done, 1)

            def in_unit(u, k, ready=None):
                if not isinstance(u, int) or u > 2:
                    pe.wait_ge(evac, u - 2)
                unit(u, k, Gh, Gl, acc[k][:, 0:NT], range(KT), ready=ready)

            def norm_stat(e):
                pe.wait_ge(ssq_ready, KT * (e + 1))
                if e == 0:
                    pe.wait_ge(consts, 1)
                nc.tensor.matmul(stat[:, 0:NT], ones[:, :], ssq[:, :], start=True, stop=True).then_inc(stat_done, 1)

            def ln_stat_sum(n):
                pe.wait_ge(ln_sum, n)
                nc.tensor.matmul(stat[:, 0:NT], ones[:, :], ssq[:, :], start=True, stop=True).then_inc(ln_stat, 1)

            def first_body(name, l, e):
                u0 = START[name, l]
                in_unit(u0, 0, (g_ready, KT * e))
                norm_stat(e)
                for k in range(1, 4):
                    in_unit(u0 + k, k)

            def more_bodies(name, l, first, end):
                u0 = START[name, l]
                with pe.Fori(first, end) as b:
                    for k in range(4):
                        in_unit(b * 4 + (u0 + k), k)

            def out_phase(name, l, tiles_of):
                u0, h0 = START[name, l], htile(l, False)
                for m in range(KT):
                    pe.wait_ge(evac, u0 + m - 2)
                    unit(u0 + m, m % 4, Hh, Hl, acc[m % 4][:, 0:NT], tiles_of(m), ready=(h_ready, h0))

            def down_phase(l):
                u0, h0 = START["f_down", l], htile(l, True)

                def out_tile(u, i, free, ready=None):
                    pe.wait_ge(evac, free)
                    for q, (a, z) in enumerate(PARTS):
                        unit(u + q, q, Hh, Hl, acc[i][:, 0:NT], range(a, z), q == 0, q == 3, ready)

                out_tile(u0, 0, u0 - 3, (h_ready, h0))
                out_tile(u0 + 4, 1, u0)
                with pe.Fori(1, 4) as b:
                    for i in range(2):
                        u = b * 8 + (u0 + 4 * i)
                        out_tile(u, i, u - 4)

            def ffn(l):
                first_body("f_up", l, 2 * l + 1)
                more_bodies("f_up", l, 1, 11)
                down_phase(l)

            first_body("a_in", 0, 0)
            for k in range(4):
                in_unit(4 + k, k)
            in_unit(8, 0)
            in_unit(9, 1)
            ln_stat_sum(1)
            for k in range(2, 6):
                in_unit(8 + k, k % 4)
            ln_stat_sum(2)
            for k in range(6, 8):
                in_unit(8 + k, k % 4)
            pe.wait_ge(consts, 8)

            def v_transposes(g):
                pe.wait_ge(v_ready, g + 1)
                if g >= 2:
                    pe.wait_ge(vtok_ready, g - 1)
                v, dst = tile_of(V3, g), mixb[g % 2]
                nc.tensor.transpose(dst[:, 0:128], v[:, 0:128], ident[:, :])
                nc.tensor.transpose(dst[:, 128:256], v[:, 128:256], ident[:, :])
                nc.tensor.transpose(dst[0:64, 256:384], v[:, 256:320], ident[:, :]).then_inc(vT_done, 1)

            def position_mix(g):
                pe.wait_ge(vtok_ready, g + 1)
                if g >= 1:
                    pe.wait_ge(mix_read, g)
                vt, w, dst = vtok[g % 2], wsT[:, g * 128:(g + 1) * 128], mixb[2]
                nc.tensor.matmul(dst[:, 0:128], vt[:, 0:128], w, start=True, stop=True)
                nc.tensor.matmul(dst[:, 128:256], vt[:, 128:256], w, start=True, stop=True)
                nc.tensor.matmul(dst[:, 256:320], vt[0:64, 256:384], wbd[:, g * 64:(g + 1) * 64],
                                 start=True, stop=True).then_inc(mixed, 1)

            v_transposes(0)
            for g in range(KT):
                if g + 1 < KT:
                    v_transposes(g + 1)
                position_mix(g)
            out_phase("a_out", 0, lambda m: range(KT))
            ffn(0)
            if layers > 1:
                norm_stat(2)
                out_phase("b_grp", 1, lambda m: (m // 2 * 2, m // 2 * 2 + 1))
                ffn(1)
            if layers > 2:
                u0 = START["c_pw1", 2]

                def conv_taps_of(m, i):
                    pe.wait_ge(z_ready, m + 1)
                    pe.wait_ge(diag_ready, m + 1)
                    if not isinstance(m, int) or m >= 2:
                        pe.wait_ge(conv_read, m - 1)
                    z, at = tile_of(zpad, m, CW), padded_at(30)
                    zs = z[:, at:at + NB * 38].rearrange("p (b t) -> p b t", b=NB)
                    for part in range(2):
                        for n in range(PETAPS):
                            k = DVETAPS + n
                            src = zs[:, :, k:k + DEC] if part else z[:, k:k + SEQ]
                            dst = sample(mixb[i]) if part else prompt(mixb[i])
                            ins = nc.tensor.matmul(dst, diag[i][:, n * P:(n + 1) * P], src,
                                                   start=n == 0, stop=n == PETAPS - 1)
                    ins.then_inc(conv_done, 1)

                in_unit(u0, 0, (g_ready, KT * 4))
                norm_stat(4)
                in_unit(u0 + 1, 1)
                in_unit(u0 + 2, 2)
                in_unit(u0 + 3, 3)
                conv_taps_of(0, 0)
                with pe.Fori(1, 4) as b:
                    for i in range(2):
                        for k in range(2 * i, 2 * i + 2):
                            in_unit(b * 4 + (u0 + k), k)
                        conv_taps_of(b * 2 + (i - 1), 1 - i)
                conv_taps_of(7, 1)
                ln_stat_sum(3)
                ln_stat_sum(4)
                out_phase("c_pw2", 2, lambda m: range(KT))
                ffn(2)
            if layers > 3:
                u0 = START["d_ab", 3]
                pe.wait_ge(evac, u0)
                for q in range(4):
                    unit(u0 + q, q, Gh, Gl, acc[0][:, 0:NT], range(2 * q, 2 * q + 2), q == 0, q == 3, (g_ready, 48))
                norm_stat(6)
                pe.wait_ge(consts, ZEROS)

                def l2_sum(n, i):
                    pe.wait_ge(l2sq_ready, n + 1)
                    for c in range(3):
                        at = n + 16 * c
                        dst = mixb[0][:, at:at + 1] if isinstance(at, int) else mixb[0][:, bass.ds(at, 1)]
                        ins = nc.tensor.matmul(dst, sq[i][:, c * P:(c + 1) * P], ones[:, 0:1], start=True, stop=True)
                    ins.then_inc(l2sums, 1)

                def turn(dst, src, n=3, w=P):
                    for c in range(n):
                        ins = nc.tensor.transpose(dst[0:w, c * P:(c + 1) * P], src[:, c * w:(c + 1) * w], ident[:, :])
                    return ins

                u0 = START["d_qk", 3]
                for k in range(4):
                    in_unit(u0 + k, k)
                    if k == 0:
                        pe.wait_ge(ab_v, G_READY)
                        turn(mixb[1], G1).then_inc(ab_t, 1)
                    if k == 3:
                        l2_sum(0, 0)
                pe.wait_ge(ab_a, GT_READY)
                for c in range(3):
                    ins = nc.tensor.matmul(mixb[2][:, c * P:(c + 1) * P], gT[:, c * P:(c + 1) * P],
                                           mincl[:, c * P:(c + 1) * P], start=True, stop=True)
                ins.then_inc(ab_t, 1)
                with pe.Fori(1, 4) as b:
                    for k in range(4):
                        in_unit(b * 4 + (u0 + k), k)
                        l2_sum(b * 4 + (k - 3), (k + 1) % 2)
                l2_sum(13, 1)
                l2_sum(14, 0)
                l2_sum(15, 1)

                pe.wait_ge(ab_v, RW_READY)
                pe.wait_ge(ab_a, RW_READY_A)
                turn(mixb[1], RW).then_inc(ab_t, 1)
                pe.wait_ge(ab_v, RN_READY)
                turn(mixb[2], rnc, w=16).then_inc(ab_t, 1)

                def gdn_pair(b):
                    u0 = START["d_vg", 3]
                    if not isinstance(b, int):
                        pe.wait_ge(ss_ready, b * 2 - 1)
                        pe.wait_ge(osd_ready, b * 2 - 1)
                    for k in range(4):
                        in_unit(b * 4 + (u0 + k), k)
                    T3 = range(3)

                    def T(ap, c, w=P):
                        return ap[:, c * P:c * P + w]

                    for x in range(2):
                        h, (ba, bb, bc, bd) = b * 2 + x, bank[4 * x:4 * x + 4]
                        if x == 0:
                            pe.wait_ge(evac, b * 4 + (u0 + 4))
                            if isinstance(b, int):
                                pe.wait_ge(ab_v, ROWS_READY)
                                pe.wait_ge(std_ready, 7)
                        pe.wait_ge(kb_ready, h + 1)
                        for c in T3:
                            nc.tensor.matmul(T(ba, c, (P, P, 64)[c]), T(kh[x], c), T(kb[x], c, (P, P, 64)[c]),
                                             start=True, stop=True)
                        for c in T3:
                            ins = nc.tensor.matmul(T(bb, c, (P, P, 64)[c]), T(kh[x], c), T(qh[x], c, (P, P, 64)[c]),
                                                   start=True, stop=True)
                        ins.then_inc(kk_done, 1)
                        turn(bc, kh[x])
                        pe.wait_ge(silu_ready, h + 17)
                        turn(bd, vf[x]).then_inc(kv_turned, 1)
                    for x in range(2):
                        pe.wait_ge(tt_ready, b * 2 + (x + 1))
                        turn(bank[4 * x], TT[x]).then_inc(t_turned, 1)
                    for lev in range(5):
                        n = 3 if lev < 2 else 2
                        for x in range(2):
                            ba = bank[4 * x]
                            if lev == 0:
                                pe.wait_ge(t_ready, b * 2 + (x + 1))
                            else:
                                pe.wait_ge(inv_ready, b * 10 + (2 * (lev - 1) + x + 1))
                            for c in range(n):
                                ins = nc.tensor.matmul(T(ba, c), T(LT[x], c), T(Tm[x], c), start=True, stop=True)
                            ins.then_inc(lt_done, 1)
                        for x in range(2):
                            bb, bc = bank[4 * x + 1:4 * x + 3]
                            pe.wait_ge(b_ready, b * 10 + (2 * lev + x + 1))
                            if lev == 0:
                                pe.wait_ge(kv_scaled, b * 2 + (x + 1))
                            for c in range(n):
                                ins = nc.tensor.matmul(T(bc, c), T(Bm[x], c), T(TT[x], c), start=True, stop=True)
                            if lev < 4:
                                for c in range(n):
                                    ins = nc.tensor.matmul(T(bb, c), T(TT[x], c), T(Bm[x], c), start=True, stop=True)
                            ins.then_inc(tb_done, 1)
                    for x in range(2):
                        ba, bb, bc, bd = bank[4 * x:4 * x + 4]
                        pe.wait_ge(inv_ready, b * 10 + (9 + x))
                        for c in T3:
                            w = (P, P, 64)[c]
                            ins = nc.tensor.matmul(T(ba, c, w), T(kw[x], c), T(TT[x], c, w), start=True, stop=True)
                        ins.then_inc(w_done, 1)
                        nc.tensor.matmul(T(bb, 0), T(TT[x], 0), T(vp[x], 0), start=True, stop=True).then_inc(u_done, 1)
                    for x in range(2):
                        h, bc, bd = b * 2 + x, bank[4 * x + 2], bank[4 * x + 3]
                        pe.wait_ge(vn_ready, b * 8 + (x + 1))
                        pe.wait_ge(qt_ready, h + 1)
                        nc.tensor.matmul(bc[:, 0:P], T(kdec[x], 0), T(VN[x], 0), start=True, stop=True).then_inc(su_done, 1)
                        nc.tensor.matmul(bd[:, 0:64], T(VN[x], 0), QT[x][:, 0:64], start=True, stop=True)
                        pe.wait_ge(w_ready, h + 1)
                        pe.wait_ge(qe_ready, h + 1)
                        pe.wait_ge(states_in[x], b * 16 + 16)
                        for s_ in range(NB):
                            rhs = WQ[x].rearrange("p (n t) -> p n t", n=2)[:, :, SEQ + s_ * DEC:SEQ + (s_ + 1) * DEC]
                            dst = bd[:, SEQ:TW].rearrange("p (n t) -> p n t", n=2)[:, :, s_ * DEC:(s_ + 1) * DEC]
                            nc.tensor.matmul(dst, SS[x][:, s_ * P:(s_ + 1) * P], rhs, start=s_ == 0, stop=False)
                        nc.tensor.matmul(bd[:, NT:TW], T(vp[x], 2), TT[x][:, SEQ:NT], start=False, stop=True)\
                            .then_inc(sv_done, 1)
                    for c in range(1, CHUNKS):
                        t0, lo = c // 2, c * CHUNK
                        for x in range(2):
                            bb, bd = bank[4 * x + 1], bank[4 * x + 3]
                            nc.tensor.matmul(T(bb, c), T(TT[x], t0), T(vp[x], t0), start=True, stop=False)
                            pe.wait_ge(s_ready, b * 8 + (2 * (c - 1) + x + 1))
                            nc.tensor.matmul(T(bb, c), WQ[x][:, NT + t0 * P:NT + (t0 + 1) * P], Sst[x],
                                             start=False, stop=True).then_inc(ws_done, 1)
                            if c == 1:
                                pe.wait_ge(vs_ready, b * 2 + (x + 1))
                            nc.tensor.matmul(bd[:, lo:lo + CHUNK], Sst[x], WQ[x][:, lo:lo + CHUNK], start=True, stop=False)
                            if c == 1:
                                nc.tensor.transpose(bank[4 * x][0:64, 0:P], vsT[x][:, 64:128], ident[:, :])\
                                    .then_inc(vs_turned, 1)
                        for x in range(2):
                            h, bc, bd = b * 2 + x, bank[4 * x + 2], bank[4 * x + 3]
                            pe.wait_ge(vn_ready, b * 8 + (2 * c + x + 1))
                            nc.tensor.matmul(bc[:, 0:P], T(kdec[x], t0), T(VN[x], c), start=True, stop=True)\
                                .then_inc(su_done, 1)
                            ins = nc.tensor.matmul(bd[:, lo:lo + CHUNK], T(VN[x], c), QT[x][:, lo:lo + CHUNK],
                                                   start=False, stop=True)
                            if c == 2:
                                pe.wait_ge(vns_ready, h + 1)
                                nc.tensor.matmul(bd[:, SEQ:NT], ident[:, :], vsT[x][:, 0:64], start=True, stop=False)
                                nc.tensor.matmul(bd[:, SEQ:NT], VNs[x], QT[x][:, SEQ:NT], start=False, stop=True)
                            if c == CHUNKS - 1:
                                ins.then_inc(o_done, 1)
                    for x in range(2):
                        h = b * 2 + x
                        pe.wait_ge(vx_ready, h + 1)
                        nc.tensor.matmul(bank[4 * x][:, :], T(kdec[x], 2), VX[x][:, 0:512], start=True, stop=True)
                        nc.tensor.matmul(bank[4 * x + 1][:, :], T(kdec[x], 2), VX[x][:, 512:1024], start=True, stop=True)\
                            .then_inc(sx_done, 1)
                    for x in range(2):
                        pe.wait_ge(osq_ready, b * 2 + (x + 1))
                        pe.wait_ge(s_ready, b * 8 + (7 + x))
                        nc.tensor.matmul(bank[4 * x + 2][:, 0:NT], ones[:, :], sq[x][:, 0:NT], start=True, stop=True)\
                            .then_inc(osum_done, 1)

                gdn_pair(0)
                with pe.Fori(1, 4) as b:
                    gdn_pair(b)
                pe.wait_ge(h_ready, htile(3, True))
                out_phase("d_out", 3, lambda m: range(KT))
                ffn(3)
            norm_stat(NORMS)

        @block.scalar
        def _(act):
            def split_hi(u, full, k, w):
                act.wait_ge(raw_full[k], full)
                if not isinstance(u, int) or u >= SLOTS:
                    act.wait_ge(unit_done, u - (SLOTS - 1))
                nc.scalar.activation(whi[k][:, 0:w], raw[k][:, 0:w], ACT.Copy).then_inc(hi_ready, 1)

            def ahead(u0, b, k, w, body=4):
                s = (k + 2) % 4
                if isinstance(b, int):
                    u = u0 + body * b + k + 2
                    if u < LAST:
                        split_hi(u, 16 * (u // 4 + 1), s, cols_of(u))
                else:
                    split_hi(b * body + (u0 + k + 2), b * (4 * body) + 16 * ((u0 + k + 2) // 4 + 1), s,
                             w or down_cols(k + 2))

            def separate(index):
                if not isinstance(index, int):
                    act.wait_ge(par_in, 16)

            def hidden_hi(t_, kt, i):
                act.wait_ge(h_mid, t_ + 1)
                separate(kt)
                nc.scalar.activation(tile_of(Hh, kt), hbuf[i][:, :], ACT.Copy).then_inc(h_hi, 1)

            def residual(e, m, i, x_ready, value):
                act.wait_ge(x_ready, value)
                if not isinstance(m, int) or e * KT + m >= 2:
                    act.wait_ge(ssq_ready, m + (e * KT - 1))
                separate(m)
                if e < NORMS:
                    nc.scalar.activation(tile_of(Gh, m), tile_of(X, m), ACT.Copy,
                                         scale=col("gain", m + e * KT)).then_inc(g_hi, 1)
                nc.scalar.activation(sq[i][:, 0:NT], tile_of(X, m), ACT.Square).then_inc(sq_ready, 1)

            def std(done, value, ready):
                act.wait_ge(done, value)
                nc.scalar.activation(sd[:, :], stat[:, 0:NT], ACT.Sqrt, scale=1.0 / D,
                                     bias=eps[:, 0:1]).then_inc(ready, 1)

            def up_body(l, b, first=False):
                u0, h0 = START["f_up", l], htile(l, True)
                for i in range(2):
                    j = b * 2 + i
                    ahead(u0, b, 2 * i, 8 * P)
                    if first and i == 0:
                        std(stat_done, 2 * l + 2, std_ready)
                    else:
                        hidden_hi(j + (h0 - 1), j - 1, 1 - i)
                    ahead(u0, b, 2 * i + 1, 8 * P)
                    act.wait_ge(tap_ready, j + (l * FT + 1))
                    if not first:
                        act.wait_ge(h_mid, j + (h0 - 1))
                    separate(j)
                    nc.scalar.activation(fsil[i][:, 0:FW - 2], ftap[i][:, 0:FW - 2], ACT.Silu,
                                         bias=col("f", j * 4 + (l * FT * 4 + 3))).then_inc(sil_ready, 1)

            def down_body(l, b):
                u0 = START["f_down", l]
                for i in range(2):
                    for q in range(4):
                        ahead(u0, b, 4 * i + q, 0, 8)
                    residual(2 * l + 2, b * 2 + i, i, evac, b * 8 + (u0 + 4 * i + 4))

            def ffn(l):
                up_body(l, 0, True)
                with act.Fori(1, 10) as b:
                    up_body(l, b)
                up_body(l, 10)
                hidden_hi(htile(l, True) + FT - 1, FT - 1, 1)
                down_body(l, 0)
                with act.Fori(1, 3) as b:
                    down_body(l, b)
                down_body(l, 3)

            def out_phase(name, l, split=0):
                u0 = START[name, l]
                for m in range(KT):
                    if m >= split:
                        ahead(u0, 0, m, 0)
                    residual(2 * l + 1, m, m % 2, evac, u0 + m + 1)

            act.wait_ge(par_in, 16)
            act.wait_ge(consts, 2)
            split_hi(0, 16, 0, UNIT)
            split_hi(1, 16, 1, UNIT)
            for m in range(KT):
                residual(0, m, m % 2, x_in, 16)
            for n in range(16):
                ahead(0, 0, n, UNIT)
                if n == 0:
                    std(stat_done, 1, std_ready)
                act.wait_ge(evac, n + 1)
                nc.scalar.activation(tile_of(V3 if n < 8 else U3, n % 8), tmp[n % 2][:, :],
                                     ACT.Gelu_apprx_tanh, bias=col("a_b", (8 + n) % 16)).then_inc(gelu_done, 1)
            std(ln_stat, 2, ln_std)
            for g in range(KT):
                act.wait_ge(vT_done, g + 1)
                if g >= 2:
                    act.wait_ge(mixed, g - 1)
                nc.scalar.activation(vtok[g % 2][:, 0:256], mixb[g % 2][:, 0:256], ACT.Copy)
                nc.scalar.activation(vtok[g % 2][0:64, 256:384], mixb[g % 2][0:64, 256:384], ACT.Copy)\
                    .then_inc(vtok_ready, 1)
                if g >= 1:
                    hidden_hi(g - 1, g - 1, (g - 1) % 2)
            hidden_hi(7, 7, 1)
            out_phase("a_out", 0)
            ffn(0)
            if layers > 1:
                std(stat_done, 3, std_ready)
                for m in range(KT):
                    hidden_hi(htile(1, False) + m, m, m % 2)
                out_phase("b_grp", 1)
                ffn(1)
            if layers > 2:
                u0 = START["c_pw1", 2]

                def glu_body(b, first=False):
                    for i in range(2):
                        m = b * 2 + i
                        ahead(u0, b, 2 * i, UNIT)
                        if first and i == 0:
                            std(stat_done, 5, std_ready)
                        ahead(u0, b, 2 * i + 1, UNIT)
                        act.wait_ge(evac, b * 4 + (u0 + 2 * i + 2))
                        separate(m)
                        nc.scalar.activation(tmb[i][:, :], tmb[i][:, :], ACT.Sigmoid,
                                             bias=col("c_b1", m * 2 + 1)).then_inc(sig_ready, 1)

                glu_body(0, True)
                with act.Fori(1, 3) as b:
                    glu_body(b)
                glu_body(3)
                std(ln_stat, 4, ln_std)
                for m in range(KT):
                    h0 = htile(2, False)
                    act.wait_ge(ca_done, m + 1)
                    act.wait_ge(h_ready, h0 + m - 1)
                    nc.scalar.activation(hbuf[m % 2][:, :], tmp[m % 2][:, :], ACT.Silu,
                                         scale=col("c_lg", m), bias=col("c_lb", m)).then_inc(h_mid, 1)
                    hidden_hi(h0 + m, m, m % 2)
                out_phase("c_pw2", 2)
                ffn(2)
            if layers > 3:
                for q in range(4):
                    ahead(START["d_ab", 3], 0, q, 0)
                std(stat_done, 7, std_ready)
                u0 = START["d_qk", 3]

                def square(n, i):
                    act.wait_ge(silu_ready, n + 1)
                    if not isinstance(n, int) or n >= 2:
                        act.wait_ge(l2sums, n - 1)
                    separate(n)
                    nc.scalar.activation(sq[i][:, 0:NT], tile_of(qk, n), ACT.Square).then_inc(l2sq_ready, 1)

                def qk_body(b, first=False):
                    for k in range(4):
                        n, i = b * 4 + k, k % 2
                        act.wait_ge(conv_taps, n + 1)
                        nc.scalar.activation(fsil[i][:, 0:QW - 3], ftap[i][:, 0:QW - 3], ACT.Tanh).then_inc(tanh_ready, 1)
                        split_hi(b * 4 + (u0 + k + 3), b * 16 + 16 * ((u0 + k + 3) // 4 + 1), (k + 3) % 4, UNIT)
                        if not first or k:
                            square(n - 1, 1 - i)
                        if first and k == 1:
                            act.wait_ge(ab_t, 1)
                            nc.scalar.activation(gT, mixb[1][:, 0:TW], ACT.Copy).then_inc(ab_a, 1)

                act.wait_ge(consts, ZEROS)
                act.wait_ge(ab_v, 1)
                nc.scalar.activation(RW[0:32, 0:NT], AB[0:32, 0:NT], ACT.Sigmoid).then_inc(ab_a, 1)
                act.wait_ge(ab_v, 2)
                nc.scalar.activation(KD[:, 0:NT], KD[:, 0:NT], ACT.Exp, scale=-1.0).then_inc(ab_a, 1)
                act.wait_ge(ab_a, 2)
                nc.scalar.activation(KD[:, 0:NT], KD[:, 0:NT], ACT.Ln, bias=ones[:, 0:1]).then_inc(ab_a, 1)
                nc.scalar.activation(dc[:, 0:1], col("d_al"), ACT.Exp).then_inc(ab_a, 1)
                split_hi(u0 + 2, 16 * (u0 // 4 + 1), 2, UNIT)
                qk_body(0, True)
                with act.Fori(1, 4) as b:
                    qk_body(b)
                square(15, 1)

                u0 = START["d_vg", 3]
                for k in range(3, 4):
                    split_hi(u0 + k, 16 * (u0 // 4 + 1), k, UNIT)

                act.wait_ge(ab_v, RW_READY)
                nc.scalar.activation(RW[EG:EG + 32, 0:NT], G1[EG:EG + 32, 0:NT], ACT.Exp).then_inc(ab_a, 1)
                nc.scalar.activation(RW[KDEC:KDEC + 32, 0:NT], KD[KDEC:KDEC + 32, 0:NT], ACT.Exp).then_inc(ab_a, 1)
                act.wait_ge(l2sums, 16)
                ns = mixb[0][:, 0:48].rearrange("p (c two) -> p c two", two=2)
                rs = rnc.rearrange("p (c two) -> p c two", two=2)
                nc.scalar.activation(rs[:, :, 0], ns[:, :, 0], ACT.Sqrt, scale=float(P), bias=dc[:, 1:2]).then_inc(ab_a, 1)
                nc.scalar.activation(rs[:, :, 1], ns[:, :, 1], ACT.Sqrt, bias=eps[:, 0:1]).then_inc(ab_a, 1)
                act.wait_ge(ab_t, 3)
                nc.scalar.activation(cols.rearrange("p (n f h) -> p n f h", n=3, f=5)[:, :, 0:4, :],
                                     mixb[1][:, 0:TW].rearrange("p (n f h) -> p n f h", n=3, f=4)[:, :, :, 0:HEADS],
                                     ACT.Copy).then_inc(ab_a, 1)

                def gdn_pair(b):
                    u0 = START["d_vg", 3]
                    for x in range(2):
                        h = b * 2 + x
                        act.wait_ge(conv_taps, h + 17)
                        nc.scalar.activation(fsil[x][:, 0:QW - 3], ftap[x][:, 0:QW - 3], ACT.Tanh).then_inc(tanh_ready, 1)
                        act.wait_ge(evac, b * 4 + (u0 + 2 * x + 2))
                        nc.scalar.activation(gtanh[x], gate[x], ACT.Tanh).then_inc(tanh_ready, 1)
                        act.wait_ge(rows_in[x], b * 48 + 48)
                        nc.scalar.activation(eg[x][:, :], gcb[x], ACT.Exp).then_inc(eg_ready, 1)
                    for x in range(2):
                        act.wait_ge(diff_ready, b * 2 + (x + 1))
                        nc.scalar.activation(dec[x][:, 0:NT], dec[x][:, 0:NT], ACT.Exp).then_inc(decay_ready, 1)
                    for x in range(2):
                        act.wait_ge(t_turned, b * 2 + (x + 1))
                        nc.scalar.activation(Tm[x], bank[4 * x][:, 0:TW], ACT.Copy).then_inc(t_ready, 1)
                    for k in range(4):
                        split_hi(b * 4 + (u0 + 4 + k), b * 16 + 16 * (u0 // 4 + 2), k, UNIT)
                    for x in range(2):
                        act.wait_ge(w_done, b * 2 + (x + 1))
                        nc.scalar.activation(WQ[x][:, NT:2 * NT], bank[4 * x][:, 0:NT], ACT.Copy, scale=-1.0)\
                            .then_inc(w_ready, 1)
                    for x in range(2):
                        act.wait_ge(o_done, b * 2 + (x + 1))
                        nc.scalar.activation(sq[x][:, 0:NT], bank[4 * x + 3][:, 0:NT], ACT.Square).then_inc(osq_ready, 1)
                    for x in range(2):
                        act.wait_ge(osum_done, b * 2 + (x + 1))
                        nc.scalar.activation(sq[x][:, 0:NT], bank[4 * x + 2][:, 0:NT], ACT.Sqrt, scale=1.0 / P,
                                             bias=eps[:, 0:1]).then_inc(osd_ready, 1)
                    for x in range(2):
                        hidden_hi(b * 2 + (htile(3, False) + x), b * 2 + x, x)

                gdn_pair(0)
                with act.Fori(1, 4) as b:
                    gdn_pair(b)
                out_phase("d_out", 3, 2)
                act.wait_ge(stored, 16 * GDN_STORED)
                ffn(3)
            std(stat_done, NORMS + 1, std_ready)

        @block.vector
        def _(dve):
            S = Steps(dve, dve_steps)
            vec = nc.vector

            def hidden_lo(t_, kt, i):
                dve.wait_ge(h_hi, t_ + 1)
                vec.tensor_tensor(tile_of(Hl, kt), hbuf[i][:, :], tile_of(Hh, kt).bitcast(F32),
                                  ALU.subtract).then_inc(h_ready, 1)

            def residual(e, m, i, first):
                if e < NORMS:
                    dve.wait_ge(g_hi, m + (e * KT + 1))
                    vec.scalar_tensor_tensor(out=tile_of(Gl, m), in0=tile_of(X, m), scalar=col("gain", m + e * KT),
                                             in1=tile_of(Gh, m).bitcast(F32), op0=ALU.mult,
                                             op1=ALU.subtract).then_inc(g_ready, 1)
                dve.wait_ge(sq_ready, m + (e * KT + 1))
                if first:
                    vec.tensor_copy(ssq[:, :], sq[i][:, 0:NT]).then_inc(ssq_ready, 1)
                else:
                    dve.wait_ge(ssq_ready, m + e * KT)
                    vec.tensor_tensor(ssq[:, :], ssq[:, :], sq[i][:, 0:NT], ALU.add).then_inc(ssq_ready, 1)

            def factor(ready, value):
                dve.wait_ge(ready, value)
                S.mark(vec.reciprocal(R[:, :], sd[:, :]))
                S.wait()

            def up_front(l, j, u, i, evacuated):
                at = padded_at(2)
                fp, ft = fpad[i], ftap[i]
                dve.wait_ge(unit_done, u + 1)
                S.wait()
                S.mark(vec.tensor_copy(in_pad(fp, 2, 0, 2), tile_of(fst, j, 16).rearrange("p (b t) -> p b t", b=NB)))
                S.mark(vec.tensor_tensor(fp[:, 2:at], prompt(acc[2 * i]), prompt(R), ALU.mult))
                vec.tensor_tensor(in_pad(fp, 2, 2, DEC), sample(acc[2 * i]), sample(R), ALU.mult).then_inc(evac, 1)
                dve.wait_ge(evac, evacuated)
                S.wait()
                new = tile_of(fnew, j, 18)
                S.mark(vec.tensor_copy(new[:, 0:2], fp[:, SEQ:SEQ + 2]))
                S.mark(vec.tensor_copy(new[:, 2:18].rearrange("p (b t) -> p b t", b=NB), in_pad(fp, 2, DEC, 2)))
                w = j * 4 + l * FT * 4
                n = FW - 2
                S.mark(vec.tensor_scalar(ft[:, 0:n], fp[:, 0:n], col("f", w), None, ALU.mult))
                S.wait()
                S.mark(vec.scalar_tensor_tensor(out=ft[:, 0:n], in0=fp[:, 1:n + 1], scalar=col("f", w + 1),
                                                in1=ft[:, 0:n], op0=ALU.mult, op1=ALU.add))
                S.wait()
                vec.scalar_tensor_tensor(out=ft[:, 0:n], in0=fp[:, 2:n + 2], scalar=col("f", w + 2),
                                         in1=ft[:, 0:n], op0=ALU.mult, op1=ALU.add).then_inc(tap_ready, 1)

            def up_mid(l, j, i, skip=False):
                t_ = j + htile(l, True)
                dve.wait_ge(sil_ready, j + (l * FT + 1))
                dve.wait_ge(h_ready, t_ - 1)
                dve.wait_ge(evac, j * 2 + (START["f_up", l] + 2))
                S.mark(vec.tensor_tensor(prompt(hbuf[i]), prompt(tmp[i]), fsil[i][:, 0:SEQ], ALU.mult))
                at = padded_at(2)
                sil = fsil[i][:, at:at + NB * 10].rearrange("p (b t) -> p b t", b=NB)[:, :, 0:DEC]
                vec.tensor_tensor(sample(hbuf[i]), sample(tmp[i]), sil, ALU.mult).then_inc(h_mid, 1)

            def up_body(l, b, first=False):
                u0, h0 = START["f_up", l], htile(l, True)
                for i in range(2):
                    j = b * 2 + i
                    lag = not (first and i == 0)
                    if lag:
                        up_mid(l, j - 1, 1 - i)
                    u = b * 4 + (u0 + 2 * i)
                    if first and i == 0:
                        dve.wait_ge(fst_in, 16 * (l + 1))
                    up_front(l, j, u, i, u + 1)
                    dve.wait_ge(unit_done, u + 2)
                    if not first:
                        dve.wait_ge(h_mid, j + (h0 - 1))
                    vec.tensor_tensor(tmp[i][:, :], acc[2 * i + 1][:, 0:NT], R[:, :], ALU.mult).then_inc(evac, 1)
                    if lag:
                        hidden_lo(j + (h0 - 1), j - 1, 1 - i)

            def down_body(l, b, first=False):
                u0 = START["f_down", l]
                for i in range(2):
                    m = b * 2 + i
                    dve.wait_ge(unit_done, b * 8 + (u0 + 4 * i + 4))
                    vec.tensor_tensor(tile_of(X, m), acc[i][:, 0:NT], tile_of(X, m), ALU.add).then_inc(evac, 4)
                    residual(2 * l + 2, m, i, first and i == 0)

            def ffn(l):
                factor(std_ready, 2 * l + 2)
                up_body(l, 0, True)
                S_PER = 2 * 7
                with dve.Fori(1, 11) as b:
                    S.enter(b, 1, S_PER)
                    up_body(l, b)
                S.leave(1, 10)
                up_mid(l, FT - 1, 1)
                hidden_lo(htile(l, True) + FT - 1, FT - 1, 1)
                down_body(l, 0, True)
                with dve.Fori(1, 4) as b:
                    down_body(l, b)

            def out_phase(name, l, add):
                u0 = START[name, l]
                for m in range(KT):
                    dve.wait_ge(unit_done, u0 + m + 1)
                    add(m, acc[m % 4][:, 0:NT], tile_of(X, m)).then_inc(evac, 1)
                    residual(2 * l + 1, m, m % 2, m == 0)

            def plain_add(m, ps, x):
                return vec.tensor_tensor(x, ps, x, ALU.add)

            def layernorm_sum(m, last, src):
                S.wait()
                op = vec.tensor_copy(ssq[:, :], src) if isinstance(m, int) and m == 0 else vec.tensor_tensor(ssq[:, :], ssq[:, :], src, ALU.add)
                if last:
                    op.then_inc(ln_sum, 1)
                else:
                    S.mark(op)

            def centre(buf, n):
                dve.wait_ge(ln_stat, 2 * n + 1)
                S.mark(vec.tensor_scalar(tmb[0][:, :], stat[:, 0:NT], 1.0 / D, None, ALU.mult))

            def centred_square(buf, m):
                S.wait()
                S.mark(vec.tensor_tensor(tile_of(buf, m), tile_of(buf, m), tmb[0][:, :], ALU.subtract))
                S.wait()
                S.mark(vec.tensor_tensor(tmb[1][:, :], tile_of(buf, m), tile_of(buf, m), ALU.mult))
                layernorm_sum(m, m == KT - 1, tmb[1][:, :])

            dve.wait_ge(par_in, 16)
            dve.wait_ge(x_in, 16)
            for m in range(KT):
                residual(0, m, m % 2, m == 0)
            factor(std_ready, 1)
            for n in range(16):
                dve.wait_ge(unit_done, n + 1)
                if n >= 2:
                    dve.wait_ge(gelu_done, n - 1)
                vec.tensor_tensor(tmp[n % 2][:, :], acc[n % 4][:, 0:NT], R[:, :], ALU.mult).then_inc(evac, 1)
                if 1 <= n <= 8:
                    dve.wait_ge(gelu_done, n)
                    layernorm_sum(n - 1, n == 8, tile_of(V3, n - 1))
                if n == 10:
                    centre(V3, 0)
                if 10 <= n <= 13:
                    centred_square(V3, 2 * (n - 10))
                    centred_square(V3, 2 * (n - 10) + 1)
            factor(ln_std, 1)

            def norm_v(g):
                v = tile_of(V3, g)
                S.mark(vec.tensor_tensor(v, v, R[:, :], ALU.mult))
                S.wait()
                vec.tensor_scalar(v, v, col("a_lg", g), col("a_lb", g), ALU.mult, ALU.add).then_inc(v_ready, 1)

            norm_v(0)
            norm_v(1)
            for g in range(KT):
                if g + 2 < KT:
                    norm_v(g + 2)
                dve.wait_ge(mixed, g + 1)
                if g == 0:
                    dve.wait_ge(mix_in, 48)
                    dve.wait_ge(gelu_done, 16)
                bs = bsb[:, g * 128:(g + 1) * 128]
                if g >= 1:
                    S.wait()
                S.mark(vec.tensor_tensor(prompt(tmp[g % 2]).rearrange("p (n t) -> p n t", n=2),
                                         prompt(mixb[2]).rearrange("p (n t) -> p n t", n=2),
                                         bs.rearrange("p (n t) -> p n t", n=1).to_broadcast([P, 2, 128]), ALU.add))
                vec.tensor_tensor(sample(tmp[g % 2]), sample(mixb[2]),
                                  bs[:, 0:DEC].rearrange("p (n t) -> p n t", n=1).to_broadcast([P, NB, DEC]),
                                  ALU.add).then_inc(mix_read, 1)
                dve.wait_ge(mix_read, g + 1)
                if g >= 2:
                    dve.wait_ge(h_ready, g - 1)
                vec.tensor_tensor(hbuf[g % 2][:, :], tmp[g % 2][:, :], tile_of(U3, g), ALU.mult).then_inc(h_mid, 1)
                hidden_lo(g, g, g % 2)
            out_phase("a_out", 0, plain_add)
            ffn(0)

            if layers > 1:
                factor(std_ready, 3)
                dve.wait_ge(pool_in, 16)
                dve.wait_ge(consts, 10)
                h0, at = htile(1, False), padded_at(15)
                for m in range(KT):
                    i, w = m % 2, POOLW[m // 2]
                    h_, x, g = hp[i], tile_of(X, m), col("gain", 2 * KT + m)
                    S.wait()
                    S.mark(vec.tensor_copy(in_pad(h_, 15, 0, 15), tile_of(pst, m, 120).rearrange("p (b t) -> p b t", b=NB)))
                    S.mark(vec.scalar_tensor_tensor(out=h_[:, 15:at], in0=prompt(x), scalar=g, in1=prompt(R),
                                                    op0=ALU.mult, op1=ALU.mult))
                    S.mark(vec.scalar_tensor_tensor(out=in_pad(h_, 15, 15, DEC), in0=sample(x), scalar=g, in1=sample(R),
                                                    op0=ALU.mult, op1=ALU.mult))
                    S.wait()
                    new = tile_of(pnew, m, 135)
                    S.mark(vec.tensor_copy(new[:, 0:15], h_[:, SEQ:SEQ + 15]))
                    S.mark(vec.tensor_copy(new[:, 15:135].rearrange("p (b t) -> p b t", b=NB), in_pad(h_, 15, DEC, 15)))
                    src, size, n = h_, 2, 0
                    while size <= w:
                        dst = lv[n % 2]
                        S.mark(vec.tensor_tensor(dst[:, size - 1:PW], src[:, size - 1:PW],
                                                 src[:, size - 1 - size // 2:PW - size // 2], ALU.add))
                        S.wait()
                        src, size, n = dst, size * 2, n + 1
                    hb = hbuf[i]
                    dve.wait_ge(h_ready, h0 + m - 1)
                    S.mark(vec.tensor_tensor(tmb[0][:, 0:16], src[:, 15:31], par[:, COL["inv"] + 16 * (m // 2):COL["inv"] + 16 * (m // 2) + 16], ALU.mult))
                    S.mark(vec.scalar_tensor_tensor(out=hb[:, 16:SEQ], in0=src[:, 31:at], scalar=1.0 / w, in1=h_[:, 31:at],
                                                    op0=ALU.mult, op1=ALU.subtract))
                    S.mark(vec.scalar_tensor_tensor(out=sample(hb), in0=in_pad(src, 15, 15, DEC), scalar=1.0 / w,
                                                    in1=in_pad(h_, 15, 15, DEC), op0=ALU.mult, op1=ALU.subtract))
                    S.wait()
                    vec.tensor_tensor(hb[:, 0:16], tmb[0][:, 0:16], h_[:, 15:31], ALU.subtract).then_inc(h_mid, 1)
                    if m >= 1:
                        hidden_lo(h0 + m - 1, m - 1, 1 - i)
                hidden_lo(h0 + 7, 7, 1)
                out_phase("b_grp", 1, lambda m, ps, x: vec.scalar_tensor_tensor(
                    out=x, in0=ps, scalar=col("b_scale", m), in1=x, op0=ALU.mult, op1=ALU.add))
                ffn(1)

            if layers > 2:
                factor(std_ready, 5)
                u0, at = START["c_pw1", 2], padded_at(30)
                dve.wait_ge(conv_in, 16 * KT)
                dve.wait_ge(consts, 11)

                def glu_body(b, first=False):
                    for i in range(2):
                        m = b * 2 + i
                        u = b * 4 + (u0 + 2 * i)
                        dve.wait_ge(unit_done, u + 1)
                        if not first:
                            dve.wait_ge(z_ready, m - 1)
                        vec.tensor_tensor(tmp[i][:, :], acc[2 * i][:, 0:NT], R[:, :], ALU.mult).then_inc(evac, 1)
                        dve.wait_ge(unit_done, u + 2)
                        vec.tensor_tensor(tmb[i][:, :], acc[2 * i + 1][:, 0:NT], R[:, :], ALU.mult).then_inc(evac, 1)
                        dve.wait_ge(sig_ready, m + 1)
                        z = tile_of(zpad, m, CW)
                        zs = z[:, at:at + NB * 38].rearrange("p (b t) -> p b t", b=NB)
                        S.mark(vec.scalar_tensor_tensor(out=z[:, 30:at], in0=prompt(tmp[i]), scalar=col("c_b1", m * 2),
                                                        in1=prompt(tmb[i]), op0=ALU.add, op1=ALU.mult))
                        vec.scalar_tensor_tensor(out=zs[:, :, 30:38], in0=sample(tmp[i]), scalar=col("c_b1", m * 2),
                                                 in1=sample(tmb[i]), op0=ALU.add, op1=ALU.mult).then_inc(z_ready, 1)
                        dve.wait_ge(z_ready, m + 1)
                        S.wait()
                        o = tile_of(Z3, m)
                        for k in range(DVETAPS):
                            w = col("c_dw", m * CONVW + k)
                            parts = ((prompt(o), z[:, k:k + SEQ]), (sample(o), zs[:, :, k:k + DEC]))
                            for dst, src in parts:
                                if k == 0:
                                    ins = vec.tensor_scalar(dst, src, w, col("c_bdw", m), ALU.mult, ALU.add)
                                else:
                                    S.wait(1)
                                    ins = vec.scalar_tensor_tensor(out=dst, in0=src, scalar=w, in1=dst,
                                                                   op0=ALU.mult, op1=ALU.add)
                                S.mark(ins)
                        if not (first and i == 0):
                            conv_sum(m - 1, 1 - i)

                def conv_sum(m, i):
                    dve.wait_ge(conv_done, m + 1)
                    S.wait()
                    z = tile_of(Z3, m)
                    vec.tensor_tensor(z, z, mixb[i][:, 0:NT], ALU.add).then_inc(conv_read, 1)
                    dve.wait_ge(conv_read, m + 1)
                    layernorm_sum(m, isinstance(m, int) and m == KT - 1, z)

                glu_body(0, True)
                with dve.Fori(1, 4) as b:
                    S.enter(b, 1, 2 * (2 + 2 * DVETAPS))
                    glu_body(b)
                S.leave(1, 3)
                conv_sum(7, 1)
                centre(Z3, 1)
                for m in range(KT):
                    centred_square(Z3, m)
                factor(ln_std, 2)
                h0 = htile(2, False)
                for m in range(KT):
                    if m >= 2:
                        dve.wait_ge(h_mid, h0 + m - 1)
                    vec.tensor_tensor(tmp[m % 2][:, :], tile_of(Z3, m), R[:, :], ALU.mult).then_inc(ca_done, 1)
                    if m >= 1:
                        hidden_lo(h0 + m - 1, m - 1, (m - 1) % 2)
                hidden_lo(h0 + 7, 7, 1)
                out_phase("c_pw2", 2, lambda m, ps, x: vec.scalar_tensor_tensor(
                    out=x, in0=ps, scalar=col("c_b2", m), in1=x, op0=ALU.add, op1=ALU.add))
                ffn(2)

            if layers > 3:
                factor(std_ready, 7)
                dve.wait_ge(consts, ZEROS)
                dve.wait_ge(gdn_in, 32)
                cw = par[:, COL["d_cw"]:COL["d_cw"] + 96]
                S.mark(vec.tensor_scalar(cw, cw, 0.5, None, ALU.mult))
                S.mark(vec.memset(dc[:, 1:2], P * EPS))

                dve.wait_ge(unit_done, START["d_ab", 3] + 4)
                vec.tensor_tensor(AB[:, 0:NT], acc[0][:, 0:NT], R[:, :], ALU.mult).then_inc(evac, 4)
                dve.wait_ge(evac, START["d_ab", 3] + 4)
                vec.tensor_scalar(XG[:, 0:NT], AB[:, 0:NT], col("d_dt"), None, ALU.add).then_inc(ab_v, 1)
                dve.wait_ge(ab_v, 1)
                vec.scalar_tensor_tensor(out=KD[:, 0:NT], in0=XG[:, 0:NT], scalar=-1.0, in1=XG[:, 0:NT],
                                         op0=ALU.mult, op1=ALU.max).then_inc(ab_v, 1)

                def conv_front(u, k, i, st, between=None):
                    at, n = padded_at(3), QW - 3
                    fp, ft = fpad[i], ftap[i]
                    dve.wait_ge(unit_done, u + 1)
                    S.wait()
                    S.mark(vec.tensor_copy(in_pad(fp, 3, 0, 3), sampled(tile_of(fst, st, 24))))
                    S.mark(vec.tensor_tensor(fp[:, 3:at], prompt(acc[k]), prompt(R), ALU.mult))
                    vec.tensor_tensor(in_pad(fp, 3, 3, DEC), sample(acc[k]), sample(R), ALU.mult).then_inc(evac, 1)
                    if between:
                        between()
                    dve.wait_ge(evac, u + 1)
                    S.wait()
                    S.mark(vec.tensor_scalar(ft[:, 0:n], fp[:, 0:n], col("d_cw", st * 4), None, ALU.mult))
                    new = tile_of(fnew, st, 27)
                    S.mark(vec.tensor_copy(new[:, 0:3], fp[:, SEQ:SEQ + 3]))
                    S.mark(vec.tensor_copy(sampled(new[:, 3:27]), in_pad(fp, 3, DEC, 3)))
                    for c in range(1, 4):
                        S.wait(2 if c == 1 else 0)
                        ins = vec.scalar_tensor_tensor(out=ft[:, 0:n], in0=fp[:, c:n + c], scalar=col("d_cw", st * 4 + c),
                                                       in1=ft[:, 0:n], op0=ALU.mult, op1=ALU.add)
                        if c < 3:
                            S.mark(ins)
                    ins.then_inc(conv_taps, 1)

                def silu_out(n, i, dst):
                    at = padded_at(3)
                    S.mark(vec.scalar_tensor_tensor(out=prompt(dst), in0=fsil[i][:, 0:SEQ], scalar=1.0,
                                                    in1=ftap[i][:, 0:SEQ], op0=ALU.add, op1=ALU.mult))
                    rest = [a[:, at:at + NB * 11].rearrange("p (b t) -> p b t", b=NB)[:, :, 0:DEC]
                            for a in (fsil[i], ftap[i])]
                    vec.scalar_tensor_tensor(out=sample(dst), in0=rest[0], scalar=1.0, in1=rest[1],
                                             op0=ALU.add, op1=ALU.mult).then_inc(silu_ready, 1)

                def qk_body(b, first=False):
                    u0 = START["d_qk", 3]
                    for k in range(4):
                        n = b * 4 + k
                        def last_silu():
                            dve.wait_ge(tanh_ready, n)
                            silu_out(n - 1, 1 - k % 2, tile_of(qk, n - 1))

                        conv_front(b * 4 + (u0 + k), k, k % 2, b * 6 + (k // 2 * 3 + k % 2),
                                   None if first and k == 0 else last_silu)

                dve.wait_ge(ab_a, 4)
                S.mark(vec.scalar_tensor_tensor(out=KD[:, 0:NT], in0=XG[:, 0:NT], scalar=0.0, in1=KD[:, 0:NT],
                                                op0=ALU.max, op1=ALU.add))
                S.wait()
                vec.tensor_scalar(G1[:, 0:NT], KD[:, 0:NT], dc[:, 0:1], -1.0, ALU.mult, ALU.mult).then_inc(ab_v, 1)
                dve.wait_ge(fout, 48)
                qk_body(0, True)
                dve.wait_ge(ab_t, 2)
                S.mark(vec.tensor_copy(G1[:, 0:NT], mixb[2][:, 0:NT]))
                S.wait()
                for a, n, w in ((0, CHUNKS, CHUNK), (SEQ, NB, DEC)):
                    g = G1[:, a:a + n * w].rearrange("p (n t) -> p n t", n=n)
                    S.mark(vec.tensor_tensor(KD[:, a:a + n * w].rearrange("p (n t) -> p n t", n=n),
                                             g[:, :, w - 1:w].to_broadcast([P, n, w]), g, ALU.subtract))
                vec.tensor_copy(RW[GC:GC + 32, 0:NT], G1[GC:GC + 32, 0:NT]).then_inc(ab_v, 1)
                with dve.Fori(1, 4) as b:
                    S.enter(b, 1, 4 * 8)
                    qk_body(b)
                S.leave(1, 3)
                dve.wait_ge(tanh_ready, 16)
                silu_out(15, 1, tile_of(qk, 15))

                dve.wait_ge(ab_a, 9)
                vec.reciprocal(rnc, rnc).then_inc(ab_v, 1)
                dve.wait_ge(ab_t, 4)
                S.mark(vec.tensor_copy(RN[0:16, 0:NT], mixb[2][0:16, 0:NT]))
                dve.wait_ge(ab_a, 10)
                S.wait()
                c3 = tile3(cols)
                vec.tensor_tensor(c3[:, :, C_BEG:C_BEG + HEADS], c3[:, :, C_BETA:C_BETA + HEADS],
                                  c3[:, :, C_EG:C_EG + HEADS],
                                  ALU.mult).then_inc(ab_v, 1)
                dve.wait_ge(ab_v, ROWS_READY)
                dve.wait_ge(rows_stored, 48)

                def gdn_pair(b):
                    u0 = START["d_vg", 3]

                    def column(name, h):
                        return c3[:, :, name + h:name + h + 1] if isinstance(h, int) else c3[:, :, bass.ds(h + name, 1)]

                    for x in range(2):
                        h = b * 2 + x
                        st = b * 6 + (x * 3 + 2)
                        conv_front(b * 4 + (u0 + 2 * x), 2 * x, x, st)
                        dve.wait_ge(unit_done, b * 4 + (u0 + 2 * x + 2))
                        vec.scalar_tensor_tensor(out=gate[x], in0=acc[2 * x + 1][:, 0:NT], scalar=0.5, in1=R[:, :],
                                                 op0=ALU.mult, op1=ALU.mult).then_inc(evac, 1)
                    for x in range(2):
                        h = b * 2 + x
                        dve.wait_ge(tanh_ready, b * 4 + (16 + 2 * (x + 1)))
                        silu_out(None, x, vf[x])
                        S.mark(vec.scalar_tensor_tensor(out=gate[x], in0=gtanh[x], scalar=1.0, in1=gate[x],
                                                        op0=ALU.add, op1=ALU.mult))
                        dve.wait_ge(rows_in[x], b * 48 + 48)
                        S.mark(vec.tensor_tensor(kh[x][:, 0:NT], tile_of(qk, h * 2 + 1), rkb[x], ALU.mult))
                        vec.tensor_tensor(qh[x][:, 0:NT], tile_of(qk, h * 2), rqb[x], ALU.mult).then_inc(kq_ready, 1)
                        dve.wait_ge(silu_ready, h + 17)
                        S.wait()
                        for c in range(3):
                            a, z = c * P, min((c + 1) * P, NT)
                            k_ = h + (c * 5 * HEADS + C_GC)
                            sc = cols[:, k_:k_ + 1] if isinstance(h, int) else cols[:, bass.ds(k_, 1)]
                            ins = vec.tensor_scalar(dec[x][:, a:z], gcb[x][:, a:z], sc, 0.0, ALU.subtract, ALU.min)
                            if c < 2:
                                S.mark(ins)
                        ins.then_inc(diff_ready, 1)
                    for x in range(2):
                        h, (ba, bb, bc, bd) = b * 2 + x, bank[4 * x:4 * x + 4]
                        dve.wait_ge(kk_done, h + 1)
                        dve.wait_ge(decay_ready, h + 1)
                        S.wait()
                        S.mark(vec.tensor_tensor(LT[x][:, 0:NT], ba[:, 0:NT], dec[x][:, 0:NT], ALU.mult))
                        vec.tensor_tensor(QT[x], bb[:, 0:NT], dec[x][:, 0:NT], ALU.mult).then_inc(scores_ready, 1)
                        dve.wait_ge(kv_turned, h + 1)
                        dve.wait_ge(qe_ready, h + 1)
                        for dst, src, name in ((vp[x], bd, C_BETA), (kw[x], bc, C_BEG), (kdec[x], bc, C_KDEC)):
                            ins = vec.tensor_tensor(tile3(dst), tile3(src[:, 0:TW]), column(name, h).to_broadcast([P, 3, P]),
                                                    ALU.mult)
                            if name == C_KDEC:
                                ins.then_inc(kv_scaled, 1)
                            else:
                                S.mark(ins)
                    for x in range(2):
                        h = b * 2 + x
                        dve.wait_ge(lt_ready, h + 1)
                        S.mark(vec.tensor_tensor(tile3(Bm[x]), tile3(LT[x]), bcast(mlev[0], 3, P), ALU.mult))
                        S.wait()
                        vec.tensor_tensor(tile3(TT[x]), bcast(ident[:, :], 3, P), tile3(Bm[x]), ALU.subtract)\
                            .then_inc(tt_ready, 1)
                    for lev in range(5):
                        n = 3 if lev < 2 else 2
                        w = n * P
                        for x in range(2):
                            dve.wait_ge(lt_done, b * 10 + (2 * lev + x + 1))
                            vec.tensor_tensor(Bm[x][:, 0:w].rearrange("p (n t) -> p n t", n=n),
                                              bank[4 * x][:, 0:w].rearrange("p (n t) -> p n t", n=n),
                                              bcast(mlev[lev + 1], n, P), ALU.mult).then_inc(b_ready, 1)
                        for x in range(2):
                            dve.wait_ge(tb_done, b * 10 + (2 * lev + x + 1))
                            if lev < 4:
                                S.mark(vec.tensor_tensor(Tm[x][:, 0:w], Tm[x][:, 0:w], bank[4 * x + 1][:, 0:w], ALU.subtract))
                            vec.tensor_tensor(TT[x][:, 0:w], TT[x][:, 0:w], bank[4 * x + 2][:, 0:w], ALU.subtract)\
                                .then_inc(inv_ready, 1)
                    for c in range(CHUNKS):
                        r = c % 2 * CHUNK
                        for x in range(2):
                            if c == 0:
                                dve.wait_ge(u_done, b * 2 + (x + 1))
                            else:
                                dve.wait_ge(ws_done, b * 6 + (2 * (c - 1) + x + 1))
                            vec.tensor_copy(VN[x][r:r + CHUNK, c * P:(c + 1) * P],
                                            bank[4 * x + 1][r:r + CHUNK, c * P:(c + 1) * P]).then_inc(vn_ready, 1)
                        for x in range(2):
                            bc = bank[4 * x + 2]
                            dve.wait_ge(su_done, b * 8 + (2 * c + x + 1))
                            if c == 0:
                                vec.tensor_copy(Sst[x], bc[:, 0:P]).then_inc(s_ready, 1)
                            else:
                                at = c * CHUNK + CHUNK - 1
                                dve.wait_ge(s_ready, b * 8 + (2 * (c - 1) + x + 1))
                                vec.scalar_tensor_tensor(out=Sst[x], in0=Sst[x], scalar=eg[x][:, at:at + 1], in1=bc[:, 0:P],
                                                         op0=ALU.mult, op1=ALU.add).then_inc(s_ready, 1)
                        for x in range(2):
                            h = b * 2 + x
                            if c == 0:
                                dve.wait_ge(sv_done, h + 1)
                                vec.tensor_copy(vsT[x], bank[4 * x + 3][:, SEQ:TW]).then_inc(vs_ready, 1)
                            if c == 1:
                                dve.wait_ge(vs_turned, h + 1)
                                vec.tensor_copy(VNs[x][0:64, :], bank[4 * x][0:64, 0:P]).then_inc(vns_ready, 1)
                    for x in range(2):
                        h = b * 2 + x
                        dve.wait_ge(osq_ready, h + 1)
                        S.mark(vec.scalar_tensor_tensor(out=gate[x], in0=bank[4 * x + 3][:, 0:NT], scalar=col("d_on"),
                                                        in1=gate[x], op0=ALU.mult, op1=ALU.mult))
                    for x in range(2):
                        h = b * 2 + x
                        dve.wait_ge(sx_done, h + 1)
                        dve.wait_ge(sdec_ready, h + 1)
                        S.mark(vec.tensor_tensor(SS[x][:, 0:512], SS[x][:, 0:512], bank[4 * x][:, :], ALU.add))
                        vec.tensor_tensor(SS[x][:, 512:1024], SS[x][:, 512:1024], bank[4 * x + 1][:, :], ALU.add)\
                            .then_inc(ss_ready, 1)
                    for x in range(2):
                        h = b * 2 + x
                        dve.wait_ge(osd_ready, h + 1)
                        S.mark(vec.reciprocal(sq[x][:, 0:NT], sq[x][:, 0:NT]))
                        S.wait()
                        dve.wait_ge(h_ready, h + (htile(3, False) - 1))
                        vec.tensor_tensor(hbuf[x][:, :], gate[x], sq[x][:, 0:NT], ALU.mult).then_inc(h_mid, 1)
                    for x in range(2):
                        hidden_lo(b * 2 + (htile(3, False) + x), b * 2 + x, x)

                gdn_pair(0)
                with dve.Fori(1, 4) as b:
                    S.enter(b, 1, PAIR_STEPS)
                    gdn_pair(b)
                S.leave(1, 3)
                out_phase("d_out", 3, plain_add)
                dve.wait_ge(stored, 16 * GDN_STORED)
                ffn(3)

            factor(std_ready, NORMS + 1)
            for m in range(KT):
                x = tile_of(X, m)
                vec.scalar_tensor_tensor(out=x, in0=x, scalar=col("gain", 8 * KT + m), in1=R[:, :],
                                         op0=ALU.mult, op1=ALU.mult).then_inc(y_ready, 1)


def lay_out(i):
    import numpy as np

    def chan(a):
        a = np.asarray(a, np.float32)
        a = a.reshape(a.shape[0] // P, P, -1)
        return np.ascontiguousarray(a.transpose(1, 0, 2).reshape(P, -1))

    def units(w, order=None):
        k, m = w.shape
        w = w.reshape(k // P, P, m // P, P).transpose(2, 1, 0, 3)
        if order is not None:
            w = w[order]
        return np.ascontiguousarray(w.reshape(m // P, P, k))

    def tokens(p, s):
        return np.concatenate([p.reshape(SEQ, -1), s.reshape(NB * DEC, -1)], 0).T

    t = {"x": chan(tokens(i["x_prompt"], i["x_sample"]))}
    inter = np.arange(2 * FT).reshape(2, FT).T.reshape(-1)
    inter8 = np.arange(16).reshape(2, 8).T.reshape(-1)
    vecs = [i["norm_mix_g"][l // 2] if l % 2 == 0 else i["norm_ffn_g"][l // 2] for l in range(8)]
    vecs = [chan(v) for v in vecs] + [chan(i["norm_final_g"])]
    inv = np.zeros((4, 16), np.float32)
    for g, w in enumerate(POOLW):
        inv[g] = 1.0 / np.minimum(np.arange(16) + 1, w)
    f = np.concatenate([i["f_w_dw"], i["f_b_dw"][:, None]], 1)
    f = f.reshape(DEPTH, 4, FT, P).transpose(3, 0, 2, 1).reshape(P, -1)
    cq = i["d_w_conv"][0].reshape(4, 3, 8, P).transpose(3, 2, 1, 0).reshape(P, -1)

    def spread(v):
        a = np.zeros((4, 32), np.float32)
        a[1:4, 0:HEADS] = v
        return a.reshape(P, 1)

    parts = {
        "gain": np.concatenate(vecs, 1), "a_b": chan(i["a_b_in"][0]), "a_lg": chan(i["a_ln_g"][0]),
        "a_lb": chan(i["a_ln_b"][0]), "b_scale": chan(i["b_scale"][0]), "c_b1": chan(i["c_b_pw1"][0])[:, inter8],
        "c_dw": chan(i["c_w_dw"][0].T), "c_bdw": chan(i["c_b_dw"][0]), "c_lg": chan(i["c_ln_g"][0]),
        "c_lb": chan(i["c_ln_b"][0]), "c_b2": chan(i["c_b_pw2"][0]),
        "d_cw": cq, "d_on": i["d_o_norm_g"][0][:, None], "d_dt": spread(i["d_dt_bias"][0]),
        "d_al": spread(i["d_a_log"][0]),
        "f": f, "inv": np.broadcast_to(inv.reshape(1, -1), (P, 64)),
    }
    par = np.zeros((P, NCOL), np.float32)
    for name, a in parts.items():
        par[:, COL[name]:COL[name] + a.shape[1]] = a
    t["par"] = par
    t["a_in"] = units(i["a_w_in"][0], list(range(8, 16)) + list(range(8)))
    t["a_out"] = units(i["a_w_out"][0])
    t["a_wsT"] = np.ascontiguousarray(i["a_w_s"][0].transpose(2, 0, 1).reshape(P, -1))
    bd = np.zeros((NB, DEC, 8, NB, DEC), np.float32)
    for b in range(NB):
        bd[b, :, :, b, :] = i["a_w_s"][0][:, :DEC, :DEC].transpose(2, 0, 1)
    t["a_wbd"] = bd.reshape(64, -1)
    t["a_bs"] = np.ascontiguousarray(i["a_b_s"][0].reshape(-1))
    g = i["b_w_grp"][0].reshape(4, 2, P, 2, P).transpose(0, 3, 2, 1, 4)
    t["b_grp"] = np.ascontiguousarray(g.reshape(8, P, 2 * P))
    t["b_st"] = np.ascontiguousarray(i["state_pool"][0].reshape(NB, 15, KT, P).transpose(3, 2, 0, 1).reshape(P, -1))
    t["c_pw1"] = units(i["c_w_pw1"][0], inter8)
    t["c_pw2"] = units(i["c_w_pw2"][0])
    t["c_st"] = np.ascontiguousarray(i["state_conv"][0].reshape(NB, 30, KT, P).transpose(2, 3, 0, 1))
    w = i["d_w_ab"][0]
    ab = np.zeros((D, 4, 32), np.float32)
    ab[:, 0, 0:HEADS] = w[:, 0:HEADS]
    ab[:, 1:4, 0:HEADS] = w[:, None, HEADS:]
    t["d_ab"] = np.ascontiguousarray(units(ab.reshape(D, P)).reshape(P, 4, 2 * P).transpose(1, 0, 2))
    w = i["d_w_qkv"][0]
    qk_order = [h + 8 * j for h in range(8) for j in range(2)]
    t["d_qk"] = units(np.ascontiguousarray(w[:, :2 * HEADS * P]), qk_order)
    t["d_vg"] = units(np.concatenate([w[:, 2 * HEADS * P:], i["d_w_g"][0]], 1), qk_order)
    t["d_out"] = units(i["d_w_out"][0])
    t["d_st"] = np.ascontiguousarray(i["state_gdn_conv"][0].reshape(NB, 3, 3, HEADS, P).transpose(4, 3, 2, 0, 1)
                                     .reshape(P, -1))
    t["d_S"] = np.ascontiguousarray(i["state_gdn_S"][0].transpose(1, 2, 0, 3).reshape(HEADS, P, NB * P))
    j, q = np.arange(P)[:, None], np.arange(P)[None, :]
    lev = [((j // (2 * s) == q // (2 * s)) & (j % (2 * s) >= s) & (q % (2 * s) < s)) for s in (2, 4, 8, 16, 32)]
    lev = [(j // 2 == q // 2) & (j < q)] + lev
    pr, sa = j // CHUNK == q // CHUNK, j // DEC == q // DEC
    masks = lev + [pr & (j < q)] * 2 + [sa & (j < q)] + [pr & (j <= q)] * 2 + [sa & (j <= q)]
    masks.append(j // DEC == np.arange(NB)[None, :])
    t["d_mask"] = np.concatenate(masks, 1).astype(np.float32)
    t["f_up"] = np.stack([units(w, inter) for w in i["f_w_up"]])
    t["f_down"] = np.stack([units(w) for w in i["f_w_down"]])
    t["f_st"] = np.ascontiguousarray(i["state_ffn_conv"].reshape(DEPTH, NB, 2, FT, P).transpose(0, 4, 3, 1, 2)
                                     .reshape(DEPTH, P, -1))
    return t


def unchan(a, tiles):
    a = a.reshape((P, tiles) + a.shape[2:]) if a.ndim > 2 else a.reshape(P, tiles, -1)
    return a.swapaxes(0, 1).reshape((tiles * P,) + a.shape[2:])


OUTS = {"y": (P, KT * NT), "chunk_v": (P, KT, 192), "pool": (P, KT * 135), "conv_p": (KT, P, 30),
        "conv_s": (KT, P, NB, 30), "ffn": (DEPTH, P, FT * 18), "gdn_conv": (P, 24 * 27),
        "gdn_Sp": (HEADS, P, P), "gdn_Ss": (HEADS, P, NB * P)}


def lay_in(r):
    import numpy as np

    def whole(a, shape):
        return np.ascontiguousarray(a).reshape(shape).astype(np.float32, copy=False)

    y = r["y"].reshape(P, KT, NT).transpose(2, 1, 0).reshape(NT, D)
    cv = r["chunk_v"].transpose(2, 1, 0).reshape(192, D)
    po = r["pool"].reshape(P, KT, 1 + NB, 15).transpose(2, 3, 1, 0).reshape(1 + NB, 15, D)
    cp = r["conv_p"].transpose(2, 0, 1).reshape(30, D)
    cs = r["conv_s"].transpose(2, 3, 0, 1).reshape(NB, 30, D)
    g = r["gdn_conv"].reshape(P, HEADS, 3, 1 + NB, 3).transpose(3, 4, 2, 1, 0).reshape(1 + NB, 3, 3 * D)
    gs = r["gdn_Ss"].reshape(HEADS, P, NB, P).transpose(2, 0, 1, 3)
    f = r["ffn"].reshape(DEPTH, P, FT, 1 + NB, 2).transpose(0, 3, 4, 2, 1).reshape(DEPTH, 1 + NB, 2, DFF)
    return (whole(y[:SEQ], (1, SEQ, D)), whole(y[SEQ:], (NB, DEC, D)),
            whole(cv[:128], (1, 1, 128, D)), whole(cv[128:], (1, NB, DEC, D)),
            whole(po[0], (1, 1, 15, D)), whole(po[1:], (1, NB, 15, D)),
            whole(cp, (1, 1, 30, D)), whole(cs, (1, NB, 30, D)),
            whole(g[0], (1, 1, 3, 3 * D)), whole(g[1:], (1, NB, 3, 3 * D)),
            whole(r["gdn_Sp"], (1, 1, HEADS, P, P)), whole(gs, (1, NB, HEADS, P, P)),
            whole(f[:, :1], (DEPTH, 1, 2, DFF)), whole(f[:, 1:], (DEPTH, NB, 2, DFF)))


def kernel(**inputs):
    import numpy as _np
    import concourse.bacc as _bacc
    from concourse import mybir as _mybir
    from concourse.bass_utils import run_bass_kernel_spmd as _run

    nc = _bacc.Bacc("TRN2", target_bir_lowering=False, num_devices=1)
    t = lay_out({n: _np.asarray(a) for n, a in inputs.items()})
    args = {n: nc.dram_tensor("in_" + n, a.shape, _mybir.dt.from_np(a.dtype), kind="ExternalInput").ap()
            for n, a in t.items()}
    outs = {n: nc.dram_tensor("out_" + n, shape, _mybir.dt.float32, kind="ExternalOutput").ap()
            for n, shape in OUTS.items()}
    trunk_kernel(nc, args, outs)
    r = _run(nc, [{"in_" + n: a for n, a in t.items()}], core_ids=[0])
    return lay_in({n: r.results[0]["out_" + n] for n in OUTS})
```
